# Optimizing a Trainium2 kernel written in Bass

```python
import math
import jax
import jax.numpy as jnp
from jax import lax
import numpy as np

D_MODEL = 2048
BATCH = 1
SEQ = 256
DEPTH = 1

HEAD_DIM = 128
N_FOX_HEADS = 8
N_MOBA_HEADS = 8
FOX_WIDTH = N_FOX_HEADS * HEAD_DIM
MOBA_WIDTH = N_MOBA_HEADS * HEAD_DIM
MIX_WIDTH = FOX_WIDTH + MOBA_WIDTH
FOX_Q_BLOCK = 128
MOBA_BLOCK = 256
MOBA_TOPK = 3
MOBA_Q_CHUNK = 32
REL_BUCKETS = 32
REL_MAX_DIST = 128
N_GROUPS = 4
EXPERTS_PER_GROUP = 4
N_EXPERTS = N_GROUPS * EXPERTS_PER_GROUP
EXPERT_TOPK = 2
D_EXPERT = 512
EPS = 1e-6
NEG = -1e30

kernel_name = 'hymba_fox_moba_hmoe_layer'

def rmsnorm(x, g):
    xf = x.astype(jnp.float32)
    y = xf * lax.rsqrt(jnp.mean(xf * xf, axis=-1, keepdims=True) + EPS)
    return (y * g.astype(jnp.float32)).astype(x.dtype)

def rel_bucket(dist):
    max_exact = REL_BUCKETS // 2
    d = jnp.maximum(dist, 0)
    log_ratio = jnp.log(jnp.maximum(d, 1).astype(jnp.float32) / max_exact) / math.log(REL_MAX_DIST / max_exact)
    large = max_exact + (log_ratio * (REL_BUCKETS - max_exact)).astype(jnp.int32)
    large = jnp.minimum(large, REL_BUCKETS - 1)
    return jnp.where(d < max_exact, d, large)

def fox_attention(q, k, v, log_f):
    B, H, S, dh = q.shape
    c = jnp.cumsum(log_f, axis=-1)
    key_pos = jnp.arange(S)
    scale = dh ** -0.5

    def block(qb):
        start = qb * FOX_Q_BLOCK
        q_blk = lax.dynamic_slice_in_dim(q, start, FOX_Q_BLOCK, axis=2)
        c_blk = lax.dynamic_slice_in_dim(c, start, FOX_Q_BLOCK, axis=2)
        q_pos = start + jnp.arange(FOX_Q_BLOCK)
        s = jnp.einsum('bhqd,bhkd->bhqk', q_blk, k).astype(jnp.float32) * scale
        s = s + (c_blk[..., :, None] - c[..., None, :])
        s = jnp.where(key_pos[None, :] <= q_pos[:, None], s, NEG)
        p = jax.nn.softmax(s, axis=-1)
        return jnp.einsum('bhqk,bhkd->bhqd', p.astype(v.dtype), v)

    out = lax.map(block, jnp.arange(S // FOX_Q_BLOCK))
    return jnp.moveaxis(out, 0, 2).reshape(B, H, S, dh)

def moba_attention(q, k, v, rel_table):
    B, H, S, dh = q.shape
    nb = -(-S // MOBA_BLOCK)
    pad = nb * MOBA_BLOCK - S
    k_blocks = jnp.pad(k, ((0, 0), (0, 0), (0, pad), (0, 0))).reshape(B, H, nb, MOBA_BLOCK, dh)
    v_blocks = jnp.pad(v, ((0, 0), (0, 0), (0, pad), (0, 0))).reshape(B, H, nb, MOBA_BLOCK, dh)
    k_mean = jnp.mean(k_blocks, axis=3)
    n_sel = min(MOBA_TOPK, nb)
    scale = dh ** -0.5
    blk_off = jnp.arange(MOBA_BLOCK)
    b_ix = jnp.arange(B)[:, None, None, None]
    h_ix = jnp.arange(H)[None, :, None, None]

    def chunk(ci):
        start = ci * MOBA_Q_CHUNK
        own = start // MOBA_BLOCK
        q_c = lax.dynamic_slice_in_dim(q, start, MOBA_Q_CHUNK, axis=2)
        q_pos = start + jnp.arange(MOBA_Q_CHUNK)
        gate = jnp.einsum('bhqd,bhnd->bhqn', q_c, k_mean).astype(jnp.float32)
        gate = jnp.where(jnp.arange(nb) < own, gate, NEG)
        _, idx = lax.top_k(gate, n_sel)
        valid = idx < own
        k_sel = k_blocks[b_ix, h_ix, idx]
        v_sel = v_blocks[b_ix, h_ix, idx]
        k_own = lax.dynamic_index_in_dim(k_blocks, own, axis=2, keepdims=False)
        v_own = lax.dynamic_index_in_dim(v_blocks, own, axis=2, keepdims=False)
        pos_sel = idx[..., None] * MOBA_BLOCK + blk_off
        pos_own = own * MOBA_BLOCK + blk_off
        s_sel = jnp.einsum('bhqd,bhqkld->bhqkl', q_c, k_sel).astype(jnp.float32) * scale
        s_sel = s_sel + rel_table[h_ix[..., None], rel_bucket(q_pos[:, None, None] - pos_sel)].astype(jnp.float32)
        s_sel = jnp.where(valid[..., None], s_sel, NEG)
        s_own = jnp.einsum('bhqd,bhld->bhql', q_c, k_own).astype(jnp.float32) * scale
        s_own = s_own + rel_table[:, rel_bucket(q_pos[:, None] - pos_own[None, :])][None].astype(jnp.float32)
        s_own = jnp.where(pos_own[None, :] <= q_pos[:, None], s_own, NEG)
        s_all = jnp.concatenate([s_sel.reshape(B, H, MOBA_Q_CHUNK, n_sel * MOBA_BLOCK), s_own], axis=-1)
        p = jax.nn.softmax(s_all, axis=-1).astype(v.dtype)
        p_sel = p[..., :n_sel * MOBA_BLOCK].reshape(B, H, MOBA_Q_CHUNK, n_sel, MOBA_BLOCK)
        p_own = p[..., n_sel * MOBA_BLOCK:]
        return (jnp.einsum('bhqkl,bhqkld->bhqd', p_sel, v_sel)
                + jnp.einsum('bhql,bhld->bhqd', p_own, v_own))

    out = lax.map(chunk, jnp.arange(S // MOBA_Q_CHUNK))
    return jnp.moveaxis(out, 0, 2).reshape(B, H, S, dh)

def hier_moe(h, w_group_router, b_group_router, w_expert_router, b_expert_router, w_gate, w_up, w_down):
    B, S, D = h.shape
    t = h.reshape(B * S, D)
    g_logits = (t @ w_group_router).astype(jnp.float32) + b_group_router.astype(jnp.float32)
    p_group = jax.nn.softmax(g_logits, axis=-1)
    group = jnp.argmax(g_logits, axis=-1)
    p_top_group = jnp.take_along_axis(p_group, group[:, None], axis=-1)
    e_logits = jnp.einsum('td,dge->tge', t, w_expert_router).astype(jnp.float32) + b_expert_router.astype(jnp.float32)
    e_logits = jnp.take_along_axis(e_logits, group[:, None, None], axis=1)[:, 0]
    p_exp = jax.nn.softmax(e_logits, axis=-1)
    top_p, top_i = lax.top_k(p_exp, EXPERT_TOPK)
    top_p = top_p / jnp.sum(top_p, axis=-1, keepdims=True)
    within = jnp.sum(jax.nn.one_hot(top_i, EXPERTS_PER_GROUP, dtype=jnp.float32) * top_p[..., None], axis=1)
    combine = jax.nn.one_hot(group, N_GROUPS, dtype=jnp.float32)[:, :, None] * within[:, None, :] * p_top_group[:, :, None]
    combine = combine.reshape(-1, N_EXPERTS).astype(h.dtype)
    hid = jax.nn.silu(jnp.einsum('td,edf->tef', t, w_gate)) * jnp.einsum('td,edf->tef', t, w_up)
    y = jnp.einsum('tef,efd->td', hid * combine[:, :, None], w_down)
    return y.reshape(B, S, D)

def setup_inputs(seed: int = 0) -> dict:
    key = jax.random.key(seed)
    ks = jax.random.split(key, 20)
    f32 = jnp.float32
    L = DEPTH
    nrm = jax.random.normal
    x = nrm(ks[0], (BATCH, SEQ, D_MODEL), f32)
    attn_norm_g = 1.0 + 0.02 * nrm(ks[1], (L, D_MODEL), f32)
    w_qkv = nrm(ks[2], (L, D_MODEL, 3 * MIX_WIDTH), f32) * D_MODEL ** -0.5
    w_fg = nrm(ks[3], (L, D_MODEL, N_FOX_HEADS), f32) * (0.1 * D_MODEL ** -0.5)
    w_in = jnp.concatenate([w_qkv, w_fg], axis=-1)
    b_forget = 4.0 + 0.5 * nrm(ks[4], (L, N_FOX_HEADS), f32)
    fox_out_norm_g = 1.0 + 0.02 * nrm(ks[5], (L, FOX_WIDTH), f32)
    moba_out_norm_g = 1.0 + 0.02 * nrm(ks[6], (L, MOBA_WIDTH), f32)
    rel_bias = 0.5 * nrm(ks[7], (N_MOBA_HEADS, REL_BUCKETS), f32)
    w_out = nrm(ks[8], (L, MIX_WIDTH, D_MODEL), f32) * MIX_WIDTH ** -0.5
    ffn_norm_g = 1.0 + 0.02 * nrm(ks[9], (L, D_MODEL), f32)
    w_group_router = nrm(ks[10], (L, D_MODEL, N_GROUPS), f32) * D_MODEL ** -0.5
    b_group_router = 0.01 * nrm(ks[11], (L, N_GROUPS), f32)
    w_expert_router = nrm(ks[12], (L, D_MODEL, N_GROUPS, EXPERTS_PER_GROUP), f32) * D_MODEL ** -0.5
    b_expert_router = 0.01 * nrm(ks[13], (L, N_GROUPS, EXPERTS_PER_GROUP), f32)
    w_gate = nrm(ks[14], (L, N_EXPERTS, D_MODEL, D_EXPERT), f32) * D_MODEL ** -0.5
    w_up = nrm(ks[15], (L, N_EXPERTS, D_MODEL, D_EXPERT), f32) * D_MODEL ** -0.5
    w_down = nrm(ks[16], (L, N_EXPERTS, D_EXPERT, D_MODEL), f32) * D_EXPERT ** -0.5
    final_norm_g = 1.0 + 0.02 * nrm(ks[17], (D_MODEL,), f32)
    return {'x': x, 'attn_norm_g': attn_norm_g, 'w_in': w_in, 'b_forget': b_forget,
            'fox_out_norm_g': fox_out_norm_g, 'moba_out_norm_g': moba_out_norm_g, 'rel_bias': rel_bias,
            'w_out': w_out, 'ffn_norm_g': ffn_norm_g, 'w_group_router': w_group_router,
            'b_group_router': b_group_router, 'w_expert_router': w_expert_router,
            'b_expert_router': b_expert_router, 'w_gate': w_gate, 'w_up': w_up, 'w_down': w_down,
            'final_norm_g': final_norm_g}

def reference(x, attn_norm_g, w_in, b_forget, fox_out_norm_g, moba_out_norm_g, rel_bias, w_out, ffn_norm_g,
              w_group_router, b_group_router, w_expert_router, b_expert_router, w_gate, w_up, w_down,
              final_norm_g):
    B, S, _ = x.shape

    def to_heads(t, n):
        return t.reshape(B, S, n, HEAD_DIM).transpose(0, 2, 1, 3)

    def from_heads(t):
        return t.transpose(0, 2, 1, 3).reshape(B, S, -1)

    for l in range(DEPTH):
        h = rmsnorm(x, attn_norm_g[l])
        proj = h @ w_in[l]
        fox_qkv = proj[..., :3 * FOX_WIDTH]
        moba_qkv = proj[..., 3 * FOX_WIDTH:3 * MIX_WIDTH]
        f_logit = proj[..., 3 * MIX_WIDTH:]
        fq, fk, fv = [to_heads(t, N_FOX_HEADS) for t in jnp.split(fox_qkv, 3, axis=-1)]
        mq, mk, mv = [to_heads(t, N_MOBA_HEADS) for t in jnp.split(moba_qkv, 3, axis=-1)]
        log_f = jax.nn.log_sigmoid(f_logit.astype(jnp.float32) + b_forget[l].astype(jnp.float32)).transpose(0, 2, 1)
        fo = rmsnorm(from_heads(fox_attention(fq, fk, fv, log_f)), fox_out_norm_g[l])
        mo = rmsnorm(from_heads(moba_attention(mq, mk, mv, rel_bias)), moba_out_norm_g[l])
        x = x + jnp.concatenate([fo, mo], axis=-1) @ w_out[l]
        x = x + hier_moe(rmsnorm(x, ffn_norm_g[l]), w_group_router[l], b_group_router[l], w_expert_router[l],
                         b_expert_router[l], w_gate[l], w_up[l], w_down[l])
    return rmsnorm(x, final_norm_g)


_drawn_inputs = setup_inputs


def setup_inputs(seed=0):
    import zlib

    import numpy as np

    out = dict(_drawn_inputs(seed))
    spreads = {}
    factors = {'fox_out_norm_g': 11.647,
     'moba_out_norm_g': 11.44,
     'b_group_router': 27.175,
     'b_expert_router': 62.211,
     'final_norm_g': 7.968,
     'ffn_norm_g': 8.0}
    for name, (base, spread) in spreads.items():
        noise = np.random.default_rng([zlib.crc32(name.encode()), seed]).standard_normal(out[name].shape)
        drawn = base * np.exp(spread * noise) if base else spread * noise
        out[name] = jnp.asarray(drawn.astype(out[name].dtype))
    for name, factor in factors.items():
        out[name] = (out[name] * factor).astype(out[name].dtype)
    return out
```

```python
from contextlib import ExitStack

import numpy as np

import concourse.bass as bass
from concourse import mybir

ALU = mybir.AluOpType
ACT = mybir.ActivationFunctionType
AX = mybir.AxisListType
F32 = mybir.dt.float32
I32 = mybir.dt.int32

P = 128
T = 256
HALF = T // P
D = 2048
KD = D // P
HD = 128
HEADS = 16
FOX = 8
GROUP_H = 4
HEAD_GROUPS = HEADS // GROUP_H
NE = 16
F = 512
KF = F // P
CAP = 64
PAIRS = NE // 2
NG = 4
EG = NE // NG
EPS = 1e-6
NEG = -1e30
BUCKETS = 32
SCALE = HD ** -0.5

SLOT = 2048
RING = 12
KPS = SLOT // 512
FREE = 1

SLOTS_QKV = 3 * KD // KPS
SLOTS_IN = HEAD_GROUPS * SLOTS_QKV
SLOTS_OUT = (D // 512) * KD // KPS
SLOTS_PAIR = 2 * (2 * KD // KPS + KF * D // SLOT)
MOE0 = SLOTS_IN + SLOTS_OUT
SLOTS_PASS = PAIRS * SLOTS_PAIR
assert SLOTS_QKV == RING and SLOTS_PAIR % RING == 0

C_ID, C_TRI, C_ONE, C_STRICT, C_WIN, C_RAMP = 0, 128, 256, 384, 512, 576
C_THR, C_N = 580, 584


def constants():
    r = np.arange(P)
    table = np.zeros((P, C_N), np.float32)
    table[:, C_ID:C_ID + P] = np.eye(P)
    table[:, C_TRI:C_TRI + P] = r[:, None] <= r[None, :]
    table[:, C_ONE:C_ONE + P] = 1.0
    table[:, C_STRICT:C_STRICT + P] = r[:, None] < r[None, :]
    table[:, C_WIN:C_WIN + CAP] = np.arange(CAP)
    table[:, C_RAMP:C_RAMP + 4] = [4, 3, 2, 1]
    table[:, C_THR:C_THR + 3] = [CAP, 2 * CAP, 3 * CAP]
    dist = np.arange(-(P - 1), T)
    d = np.maximum(dist, 0)
    exact = BUCKETS // 2
    ratio = np.log(np.maximum(d, 1).astype(np.float32) / exact) / np.log(128 / exact)
    large = np.minimum(exact + (ratio * (BUCKETS - exact)).astype(np.int32), BUCKETS - 1)
    bucket = np.where(d < exact, d, large)
    onehot = np.zeros((BUCKETS + 1, 384), np.float32)
    onehot[bucket[dist >= 0], np.nonzero(dist >= 0)[0]] = 1.0
    onehot[BUCKETS, :dist.size][dist < 0] = NEG
    rows = np.arange(16)
    pick = np.zeros((16, 2 + 2 * HEADS), np.float32)
    pick[:, 0] = rows < FOX
    pick[:, 1] = rows >= FOX
    for h in range(FOX):
        pick[:, 2 + h] = rows == FOX + h
        pick[:, 2 + HEADS + h] = rows == h
    frame = np.zeros((HEADS, BUCKETS + 1), np.float32)
    frame[:, BUCKETS] = 1.0
    return table, onehot, pick, frame


def layer(nc, x_in, g_attn, w_in, b_forget, g_fox, g_moba, rel_bias, w_out, g_ffn, w_gr, b_gr, w_er, b_er,
          w_gate, w_up, w_down, g_final, table_in, onehot_in, pick_in, frame_in, out):
    ctx = ExitStack()
    with ctx:
        def sb(name, shape, dt=F32):
            return ctx.enter_context(nc.sbuf_tensor(name, shape, dt))

        def sem(name):
            return ctx.enter_context(nc.semaphore(name))

        ring = sb("ring", [P, RING, SLOT])
        x = sb("x", [P, HALF, D])
        hT = sb("hT", [P, KD, T])
        wide = sb("wide", [P, HALF, D])
        heads = sb("heads", [P, 2048])
        qT = heads[:, 0:1024].rearrange("p (a t) -> p a t", a=GROUP_H)
        kT = heads[:, 1024:2048].rearrange("p (a t) -> p a t", a=GROUP_H)
        xeT = heads[:, :].rearrange("p (k s) -> p k s", k=KD)
        rows = sb("rows", [P, 2048])
        qk_tok = rows[:, 0:1024].rearrange("p (h n) -> p h n", h=HALF)
        v_tok = rows[:, 1024:2048].rearrange("p (h n) -> p h n", h=HALF)
        y_slots = rows[:, :]
        table = sb("table", [P, C_N])
        ident, tri = table[:, C_ID:C_ID + P], table[:, C_TRI:C_TRI + P]
        tri_ones, ones = table[:, C_TRI:C_TRI + T], table[:, C_ONE:C_ONE + P]
        strict = table[:, C_STRICT:C_STRICT + P]
        window, ramp = table[:, C_WIN:C_WIN + CAP], table[:, C_RAMP:C_RAMP + 4]
        onehot = sb("onehot", [BUCKETS + 1, 384])
        pick = sb("pick", [16, 2 + 2 * HEADS])
        gains = sb("gains", [3 * KD, P])
        gT = sb("gT", [P, 3 * KD])
        gfin = sb("gfin", [P, D])
        wf = sb("wf", [P, KD, FOX])
        bf = sb("bf", [P, HALF, FOX])
        wr = sb("wr", [P, KD, NG + NE])
        rb = sb("rb", [P, HALF, NG + NE])
        rel = sb("rel", [HEADS, BUCKETS + 1])
        relT = sb("relT", [BUCKETS + 1, HEADS])
        band = sb("band", [HEADS, 384])
        band_dram = nc.dram_tensor("band_dram", [HEADS, 384], F32)
        bias = sb("bias", [P, GROUP_H, T])
        crow = sb("crow", [16, T])
        gate_q = sb("gate_q", [16, T])
        gate_k = sb("gate_k", [16, GROUP_H, T])
        lf = sb("lf", [P, HALF, 16])
        zf = sb("zf", [P, 4, 16])
        sc = sb("sc", [P, 384])
        pr = sb("pr", [P, 384])
        prT = sb("prT", [P, 384])
        nmx = sb("nmx", [P, 2])
        rsum = sb("rsum", [P, 2, 2])
        rinv = sb("rinv", [P, 2, 2])
        ssq = sb("ssq", [P, 24])
        ms = sb("ms", [P, 4])
        lnms = sb("lnms", [P, 4])
        r0 = sb("r0", [P, 4])
        r1 = sb("r1", [P, 4])
        rs = sb("rs", [P, 4])
        rt = sb("rt", [P, HALF, 160])
        mask = sb("mask", [P, HALF, NE])
        comb = sb("comb", [P, HALF, NE])
        pos = sb("pos", [P, HALF, NE])
        cmax = sb("cmax", [P, 8])
        n_pass = sb("n_pass", [1, 1], I32)
        pickD = sb("pickD", [P, HALF, 2 * CAP])
        pickW = sb("pickW", [P, HALF, 2 * CAP])
        pickWT = sb("pickWT", [P, T])
        sg = sb("sg", [P, F])
        hid = sb("hid", [P, F])
        hidT = sb("hidT", [P, KF, P])

        bank = [ctx.enter_context(nc.psum_tensor(f"bank{i}", [P, 512], F32)) for i in range(8)]

        slot_in = [sem(f"slot_in{s}") for s in range(RING)]
        slots_used = sem("slots_used")
        x_loaded, small_loaded = sem("x_loaded"), sem("small_loaded")
        gfin_loaded = sem("gfin_loaded")
        band_stored, bias_loaded = sem("band_stored"), sem("bias_loaded")
        squares = sem("squares")
        ms_ready, r0_ready, rs_ready = sem("ms_ready"), sem("r0_ready"), sem("rs_ready")
        scaled = sem("scaled")
        tr_full = sem("tr_full")
        tr_dve, tr_act = sem("tr_dve"), sem("tr_act")
        small_pe, small_dve, small_act = sem("small_pe"), sem("small_dve"), sem("small_act")
        q_moved, k_moved, v_moved = sem("q_moved"), sem("k_moved"), sem("v_moved")
        t_full, t_moved = sem("t_full"), sem("t_moved")
        s_full, s_moved = sem("s_full"), sem("s_moved")
        nmx_ready, p_ready = sem("nmx_ready"), sem("p_ready")
        rinv_ready = sem("rinv_ready")
        pv_full, o_moved = sem("pv_full"), sem("o_moved")
        gate_k_ready = sem("gate_k_ready")
        x_added = sem("x_added")
        routed_pe, pass_ready = sem("routed_pe"), sem("pass_ready")
        picks = sem("picks")
        b6_full, b6_moved, b7_full, b7_moved = sem("b6_full"), sem("b6_moved"), sem("b7_full"), sem("b7_moved")
        wt_full, wt_moved = sem("wt_full"), sem("wt_moved")
        gate_read, hid_ready = sem("gate_read"), sem("hid_ready")
        y_moved_act, y_moved_dve = sem("y_moved_act"), sem("y_moved_dve")
        out_ready, out_stored = sem("out_ready"), sem("out_stored")
        window_ready = sem("window_ready")
        dve_step, act_step = sem("dve_step"), sem("act_step")

        block = ctx.enter_context(nc.Block())

        w_in_v = w_in.rearrange("o (j k p) n -> (o p) j k n", p=P, k=KPS)
        w_out_v = w_out.rearrange("o (j k p) n -> (o p) j k n", p=P, k=KPS)
        w_gate_v = w_gate.rearrange("o e (j k p) f -> p (o e) j k f", p=P, k=KPS)
        w_up_v = w_up.rearrange("o e (j k p) f -> p (o e) j k f", p=P, k=KPS)
        w_down_v = w_down.rearrange("o e (k p) d -> p (o e) k d", p=P)

        def slot_block(s, k):
            return ring[:, s, k * 512:(k + 1) * 512]

        def moe_slot(j):
            return (MOE0 + j) % RING, (MOE0 + j) // RING

        @block.sync
        def _(sp):
            def qkv_loads(hg, first):
                for s in range(SLOTS_QKV):
                    b, j = divmod(s, KD // KPS)
                    kind, half = divmod(hg, 2) if first else (hg // 2, hg % 2)
                    col = kind * 3072 + half * 512 + b * 1024
                    if not first:
                        sp.wait_ge(slots_used, hg * SLOTS_QKV + s - RING + 1)
                    sp.dma_start(ring[:, s, :].rearrange("p (k n) -> p k n", k=KPS),
                                 w_in_v[:, j, :, bass.ds(col, 512)]).then_inc(slot_in[s], 16)

            qkv_loads(0, True)
            with sp.Fori(1, HEAD_GROUPS) as hg:
                qkv_loads(hg, False)
            for i in range(SLOTS_OUT):
                n = SLOTS_IN + i
                cb, j = divmod(i, KD // KPS)
                sp.wait_ge(slots_used, n - RING + 1)
                sp.dma_start(ring[:, n % RING, :].rearrange("p (k n) -> p k n", k=KPS),
                             w_out_v[:, j, :, cb * 512:(cb + 1) * 512]).then_inc(slot_in[n % RING], 16)

            def pair_loads(base, pair):
                j = 0
                for w, n in ((w_gate_v, KD // KPS), (w_up_v, KD // KPS), (w_down_v, KF)):
                    for c in range(n):
                        for e in range(2):
                            s, _ = moe_slot(j)
                            sp.wait_ge(slots_used, base + (j - RING + 1))
                            src = w[:, bass.ds(2 * pair + e, 1), c]
                            dst = ring[:, s, :]
                            if w is w_down_v:
                                sp.dma_start(dst, src.rearrange("p o d -> p (o d)")).then_inc(slot_in[s], 16)
                            else:
                                sp.dma_start(dst.rearrange("p (k f) -> p k f", k=KPS),
                                             src.rearrange("p o k f -> p (o k) f")).then_inc(slot_in[s], 16)
                            j += 1

            with sp.Fori(0, PAIRS) as pair:
                pair_loads(MOE0 + pair * SLOTS_PAIR, pair)
            sp.wait_ge(pass_ready, 1)
            passes = sp.value_load(n_pass[0:1, 0:1], min_val=1, max_val=T // CAP)
            with sp.If(passes > 1):
                with sp.Fori(1, passes) as p:
                    with sp.Fori(0, PAIRS) as pair:
                        pair_loads(MOE0 + p * SLOTS_PASS + pair * SLOTS_PAIR, pair)
            for h in range(HALF):
                sp.wait_ge(out_ready, h + 1)
                sp.dma_start(out[0, h * P:(h + 1) * P, :], wide[:, h, :]).then_inc(out_stored, 16)
            sp.wait_ge(out_stored, 16 * HALF)

        ROUND = 8
        PER_BANK = KD // ROUND

        def tokens_of(cols):
            return cols.rearrange("p (k t) -> p k t", k=PER_BANK)

        def bank7_uses(h):
            return 8 * h - 4

        class Own:

            def __init__(self, eng, own):
                self.eng, self.own, self.n = eng, own, 0

            def __call__(self, ins):
                self.n += 1
                ins.then_inc(self.own, 1)
                self.eng.wait_ge(self.own, self.n)

        def spread(v, n):
            return bass.AP(tensor=v.tensor, offset=0, ap=[[0, P], [0, HALF], [1, n]])

        small = [
            (table[:, :], table_in), (onehot[:, :], onehot_in), (pick[:, :], pick_in),
            (gains[0:KD, :], g_attn.rearrange("o (k p) -> (o k) p", p=P)),
            (gains[KD:KD + FOX, :], g_fox.rearrange("o (k p) -> (o k) p", p=P)),
            (gains[KD + FOX:2 * KD, :], g_moba.rearrange("o (k p) -> (o k) p", p=P)),
            (gains[2 * KD:3 * KD, :], g_ffn.rearrange("o (k p) -> (o k) p", p=P)),
            (rel[0:FOX, :], frame_in[0:FOX, :]),
            (rel[FOX:HEADS, BUCKETS:BUCKETS + 1], frame_in[FOX:HEADS, BUCKETS:BUCKETS + 1]),
            (rel[FOX:HEADS, 0:BUCKETS], rel_bias),
            (wf[:, :, :], w_in[0, :, 3 * D:].rearrange("(k p) n -> p k n", p=P)),
            (bf[:, :, :], spread(b_forget, FOX)),
            (wr[:, :, 0:NG], w_gr.rearrange("o (k p) n -> p (o k) n", p=P)),
            (wr[:, :, NG:], w_er.rearrange("o (k p) g e -> p (o k) (g e)", p=P)),
            (rb[:, :, 0:NG], spread(b_gr, NG)),
            (rb[:, :, NG:], spread(b_er, NE)),
        ]
        ALL_SMALL = 16 * len(small)

        @block.scalar
        def _(act):
            own = Own(act, act_step)
            for s in (p_ready, gate_read, y_moved_act):
                act.sem_inc(s, FREE)
            for h in range(HALF):
                act.dma_start(x[:, h, :], x_in[0, h * P:(h + 1) * P, :]).then_inc(x_loaded, 16)
            for dst, src in small:
                act.dma_start(dst, src, allow_slow_non_contiguous=(src.shape[-1] == 1)).then_inc(small_loaded, 16)
            act.dma_start(gfin[:, :], g_final.partition_broadcast(P)).then_inc(gfin_loaded, 16)

            def rsqrt_start(k, n):
                act.wait_ge(ms_ready, k)
                own(nc.scalar.activation(lnms[:, 0:n], ms[:, 0:n], ACT.Ln))
                nc.scalar.activation(r0[:, 0:n], lnms[:, 0:n], ACT.Exp, scale=-0.5).then_inc(r0_ready, 1)

            def transposed_out(u):
                for b in range(1, ROUND, 2):
                    act.wait_ge(tr_full, ROUND * u + b + 1)
                    for kk in range(PER_BANK):
                        k = PER_BANK * b + kk
                        last = nc.scalar.activation(hT[:, k, :], bank[b][:, kk * T:(kk + 1) * T], ACT.Copy,
                                                    scale=gT[:, u * KD + k:u * KD + k + 1])
                    last.then_inc(tr_act, 1)

            act.wait_ge(x_loaded, 16 * HALF)
            for h in range(HALF):
                nc.scalar.activation(wide[:, h, :], x[:, h, :], ACT.Square,
                                     accum_out=ssq[:, h:h + 1]).then_inc(squares, 1)
            rsqrt_start(1, HALF)
            act.wait_ge(rs_ready, 1)
            nc.scalar.activation(wide[:, 1, :], x[:, 1, :], ACT.Copy, scale=rs[:, 1:2]).then_inc(scaled, 1)
            act.wait_ge(small_dve, 2)
            transposed_out(0)

            act.wait_ge(small_dve, 4)
            own(nc.scalar.activation(zf[:, 3, :], zf[:, 2, :], ACT.Exp, scale=-1.0))
            nc.scalar.activation(zf[:, 2, :], zf[:, 3, :], ACT.Ln, bias=1.0).then_inc(small_act, 1)

            def step(h, qkv, attend):
                g = h - 1 if attend else None

                def exps(a):
                    act.wait_ge(nmx_ready, 4 * g + a + 1)
                    act.wait_ge(t_full, bank7_uses(h) + a)
                    if a >= 2:
                        act.wait_ge(rinv_ready, 4 * g + a - 1)
                    for qt, (lo, hi) in enumerate(((0, P), (P, 3 * P))):
                        nc.scalar.activation(pr[:, lo:hi], sc[:, lo:hi], ACT.Exp, bias=nmx[:, qt:qt + 1],
                                             accum_out=rsum[:, a % 2, qt:qt + 1]).then_inc(p_ready, 1)

                def outputs(a):
                    act.wait_ge(pv_full, FREE + 4 * g + a + 1)
                    act.wait_ge(rinv_ready, 4 * g + a + 1)
                    for half in range(HALF):
                        last = nc.scalar.activation(wide[:, half, bass.ds((4 * g + a) * HD, HD)],
                                                    bank[4 + a % 2][:, half * HD:(half + 1) * HD], ACT.Copy,
                                                    scale=rinv[:, a % 2, half:half + 1])
                    last.then_inc(o_moved, 1)

                if attend:
                    exps(0)
                    exps(1)
                    exps(2)
                    outputs(0)
                    exps(3)
                    outputs(1)
                if qkv:
                    act.wait_ge(slots_used, SLOTS_QKV * h + 4)
                    if attend:
                        act.wait_ge(t_full, bank7_uses(h))
                    for half in range(HALF):
                        nc.scalar.activation(qk_tok[:, half, :], bank[half][:, :], ACT.Copy,
                                             scale=SCALE).then_inc(q_moved, 1)
                if attend:
                    outputs(2)
                    outputs(3)
                if qkv:
                    act.wait_ge(slots_used, SLOTS_QKV * h + 12)
                    for half in range(HALF):
                        nc.scalar.activation(v_tok[:, half, :], bank[4 + half][:, :],
                                             ACT.Copy).then_inc(v_moved, 1)

            step(0, True, False)
            with act.Fori(1, HEAD_GROUPS) as h:
                step(h, True, True)
            step(HEAD_GROUPS, False, True)

            act.wait_ge(o_moved, HEADS)
            act.wait_ge(slots_used, SLOTS_IN)
            for h in range(HALF):
                for kind in range(2):
                    i = 2 * h + kind
                    nc.scalar.activation(hT[:, 4 * i:4 * i + 4, :].rearrange("p k t -> p (k t)"),
                                         wide[:, h, kind * 1024:(kind + 1) * 1024], ACT.Square,
                                         accum_out=ssq[:, 2 + i:3 + i]).then_inc(squares, 1)
            rsqrt_start(2, 4)
            act.wait_ge(rs_ready, 2)
            for kind in range(2):
                part = wide[:, 1, kind * 1024:(kind + 1) * 1024]
                nc.scalar.activation(part, part, ACT.Copy, scale=rs[:, 2 + kind:3 + kind]).then_inc(scaled, 1)
            transposed_out(1)

            for cb in range(4):
                for h in range(HALF):
                    act.wait_ge(x_added, 2 * cb + h + 1)
                    part = slice(cb * 512, (cb + 1) * 512)
                    nc.scalar.activation(wide[:, h, part], x[:, h, part], ACT.Square,
                                         accum_out=ssq[:, 8 + 4 * h + cb:9 + 4 * h + cb]).then_inc(squares, 1)
            rsqrt_start(3, HALF)
            act.wait_ge(rs_ready, 3)
            nc.scalar.activation(wide[:, 1, :], x[:, 1, :], ACT.Copy, scale=rs[:, 1:2]).then_inc(scaled, 1)
            transposed_out(2)
            act.wait_ge(small_dve, 7)
            nc.scalar.activation(rt[:, :, 4:8], rt[:, :, 0:4], ACT.Exp).then_inc(small_act, 1)
            act.wait_ge(small_dve, 8)
            nc.scalar.activation(rt[:, :, 36:40], rt[:, :, 32:36], ACT.Exp).then_inc(small_act, 1)

            act.wait_ge(pass_ready, 1)
            passes = act.value_load(n_pass[0:1, 0:1], min_val=1, max_val=T // CAP)
            with act.Fori(0, passes) as p:
                with act.Fori(0, PAIRS) as i:
                    q = p * PAIRS + i
                    base = MOE0 + q * SLOTS_PAIR
                    act.wait_ge(slots_used, base + 8)
                    act.wait_ge(hid_ready, FREE + q)
                    nc.scalar.activation(sg[:, :], bank[0][:, :], ACT.Silu).then_inc(gate_read, 1)
                    act.wait_ge(b6_full, 7 * q + 3)
                    nc.scalar.activation(hidT[:, :, :].rearrange("p k s -> p (k s)"), bank[6][:, :],
                                         ACT.Copy).then_inc(b6_moved, 1)
                    act.wait_ge(slots_used, base + SLOTS_PAIR)
                    for cb in range(2):
                        nc.scalar.activation(y_slots[:, cb * 512:(cb + 1) * 512], bank[2 + cb][:, :],
                                             ACT.Copy).then_inc(y_moved_act, 1)

            act.wait_ge(b6_moved, FREE + passes * (7 * PAIRS))
            act.wait_ge(b7_moved, FREE + passes * (6 * PAIRS))
            for h in range(HALF):
                nc.scalar.activation(wide[:, h, :], x[:, h, :], ACT.Square,
                                     accum_out=ssq[:, 18 + h:19 + h]).then_inc(squares, 1)
            rsqrt_start(4, HALF)

        @block.gpsimd
        def _(pool):
            pool.wait_ge(small_dve, 3)
            pool.dma_start(band_dram.ap(), band[:, :]).then_inc(band_stored, 16)
            pool.wait_ge(band_stored, 16)
            windows = bass.AP(tensor=band_dram, offset=0, ap=[[1, P], [384, HEADS], [1, T]])
            pool.dma_start(bias[:, :, :], windows[:, 0:GROUP_H, :]).then_inc(bias_loaded, 16)
            with pool.Fori(1, HEAD_GROUPS) as g:
                pool.wait_ge(s_moved, FREE + 4 * g)
                pool.dma_start(bias[:, :, :], windows[:, bass.ds(GROUP_H * g, GROUP_H), :]).then_inc(bias_loaded, 16)

        @block.vector
        def _(dve):
            own = Own(dve, dve_step)

            def rsqrt(k, n, sums, width):
                nc.vector.tensor_scalar(ms[:, 0:n], ssq[:, sums:sums + n], 1.0 / width, EPS, ALU.mult,
                                        ALU.add).then_inc(ms_ready, 1)
                dve.wait_ge(ms_ready, k)
                dve.wait_ge(r0_ready, k)
                own(nc.vector.tensor_tensor(r1[:, 0:n], r0[:, 0:n], r0[:, 0:n], ALU.mult))
                own(nc.vector.tensor_tensor(r1[:, 0:n], r1[:, 0:n], ms[:, 0:n], ALU.mult))
                own(nc.vector.tensor_scalar(r1[:, 0:n], r1[:, 0:n], -0.5, 1.5, ALU.mult, ALU.add))
                nc.vector.tensor_tensor(rs[:, 0:n], r0[:, 0:n], r1[:, 0:n], ALU.mult).then_inc(rs_ready, 1)
                dve.wait_ge(rs_ready, k)

            def transposed_out(u):
                for b in range(0, ROUND, 2):
                    dve.wait_ge(tr_full, ROUND * u + b + 1)
                    k = PER_BANK * b
                    nc.vector.tensor_tensor(
                        hT[:, k:k + PER_BANK, :], tokens_of(bank[b][:, :]),
                        gT[:, u * KD + k:u * KD + k + PER_BANK].unsqueeze(2).to_broadcast([P, PER_BANK, T]),
                        ALU.mult).then_inc(tr_dve, 1)

            for s in (s_moved, b6_moved, b7_moved, y_moved_dve, hid_ready):
                dve.sem_inc(s, FREE)
            dve.wait_ge(small_pe, 2)
            nc.vector.tensor_copy(gT[:, :], bank[7][:, 0:3 * KD]).then_inc(small_dve, 1)
            nc.vector.tensor_copy(relT[:, :], bank[7][0:BUCKETS + 1, 64:64 + HEADS]).then_inc(small_dve, 1)
            dve.wait_ge(small_pe, 3)
            nc.vector.tensor_copy(band[:, :], bank[7][0:HEADS, 128:512]).then_inc(small_dve, 1)
            dve.wait_ge(squares, HALF)
            rsqrt(1, HALF, 0, D)
            nc.vector.tensor_scalar(wide[:, 0, :], x[:, 0, :], rs[:, 0:1], None, ALU.mult).then_inc(scaled, 1)
            transposed_out(0)

            dve.wait_ge(small_pe, 4)
            zb, neg, mag, ln1 = zf[:, 0, :], zf[:, 1, :], zf[:, 2, :], zf[:, 2, :]
            own(nc.vector.tensor_tensor(zb, bank[6][:, 0:16], bf[:, :, :].rearrange("p h n -> p (h n)"), ALU.add))
            own(nc.vector.tensor_scalar(neg, zb, 0.0, None, ALU.min))
            nc.vector.scalar_tensor_tensor(out=mag, in0=neg, scalar=-2.0, in1=zb, op0=ALU.mult,
                                           op1=ALU.add).then_inc(small_dve, 1)
            dve.wait_ge(small_act, 1)
            halves = [v.rearrange("p (h n) -> p h n", h=HALF) for v in (neg, ln1)]
            nc.vector.tensor_tensor(lf[:, :, 0:FOX], halves[0], halves[1], ALU.subtract)
            nc.vector.tensor_tensor(lf[:, :, FOX:], halves[1], halves[0], ALU.subtract).then_inc(small_dve, 1)
            dve.wait_ge(small_pe, 5)
            own(nc.vector.tensor_copy(crow[:, :], bank[6][0:16, P:3 * P]))
            nc.vector.tensor_scalar(gate_q[:, :], crow[:, :], pick[:, 0:1], pick[:, 1:2], ALU.mult,
                                    ALU.add).then_inc(small_dve, 1)

            def step(h, qkv, attend):
                g = h - 1 if attend else None
                uses = bank7_uses(h) if attend else 0
                first = uses + 4 if attend else 0

                def scores(a):
                    dve.wait_ge(s_full, 4 * g + a + 1)
                    if a == 0:
                        dve.wait_ge(bias_loaded, 16 * (g + 1))
                    dve.wait_ge(p_ready, FREE + 2 * (4 * g + a))
                    for qt, (lo, hi) in enumerate(((0, P), (P, 3 * P))):
                        last = nc.vector.tensor_tensor(sc[:, lo:hi], bank[6][:, lo:hi],
                                                       bias[:, a, 0:hi - lo][:, ::-1], ALU.add)
                    last.then_inc(s_moved, 1)
                    dve.wait_ge(s_moved, FREE + 4 * g + a + 1)
                    for qt, (lo, hi) in enumerate(((0, P), (P, 3 * P))):
                        last = nc.vector.tensor_reduce(nmx[:, qt:qt + 1], sc[:, lo:hi], AX.X, ALU.max, negate=True)
                    last.then_inc(nmx_ready, 1)

                def probs(a):
                    dve.wait_ge(t_full, uses + a + 1)
                    dve.wait_ge(pv_full, FREE + 4 * g + a)
                    nc.vector.tensor_copy(prT[:, :], bank[7][:, 0:3 * P]).then_inc(t_moved, 1)
                    dve.wait_ge(o_moved, 4 * g + a - 1) if a >= 2 else None
                    nc.vector.reciprocal(rinv[:, a % 2, :], rsum[:, a % 2, :]).then_inc(rinv_ready, 1)

                def by_head(dst, n):
                    for part in range(2):
                        dve.wait_ge(t_full, first + n + part + 1)
                        nc.vector.tensor_copy(dst[:, 2 * part:2 * part + 2, :],
                                              tokens_of(bank[7][:, :])).then_inc(t_moved, 1)

                if attend:
                    scores(0)
                    scores(1)
                    probs(0)
                    scores(2)
                    probs(1)
                    scores(3)
                    probs(2)
                    probs(3)
                if qkv:
                    by_head(qT, 0)
                    dve.wait_ge(slots_used, SLOTS_QKV * h + 8)
                    for half in range(HALF):
                        nc.vector.tensor_copy(qk_tok[:, half, :], bank[2 + half][:, :]).then_inc(k_moved, 1)
                    by_head(kT, 2)
                    for a in range(GROUP_H):
                        last = nc.vector.tensor_scalar(
                            gate_k[:, a, :], crow[:, :], pick[:, bass.ds(2 + GROUP_H * h + a, 1)],
                            pick[:, bass.ds(2 + HEADS + GROUP_H * h + a, 1)], ALU.mult, ALU.add)
                    last.then_inc(gate_k_ready, 1)

            step(0, True, False)
            with dve.Fori(1, HEAD_GROUPS) as h:
                step(h, True, True)
            step(HEAD_GROUPS, False, True)

            dve.wait_ge(squares, HALF + 4)
            rsqrt(2, 4, 2, D // 2)
            for kind in range(2):
                part = wide[:, 0, kind * 1024:(kind + 1) * 1024]
                nc.vector.tensor_scalar(part, part, rs[:, kind:kind + 1], None, ALU.mult).then_inc(scaled, 1)
            transposed_out(1)
            for cb in range(4):
                dve.wait_ge(slots_used, SLOTS_IN + 4 * (cb + 1))
                for h in range(HALF):
                    part = x[:, h, cb * 512:(cb + 1) * 512]
                    nc.vector.tensor_tensor(part, part, bank[2 * cb + h][:, :], ALU.add).then_inc(x_added, 1)
            dve.wait_ge(squares, HALF + 4 + 8)
            own(nc.vector.tensor_reduce(ssq[:, 16:18], ssq[:, 8:16].rearrange("p (h c) -> p h c", h=HALF),
                                        AX.X, ALU.add))
            rsqrt(3, HALF, 16, D)
            nc.vector.tensor_scalar(wide[:, 0, :], x[:, 0, :], rs[:, 0:1], None, ALU.mult).then_inc(scaled, 1)
            transposed_out(2)

            TT, TR = nc.vector.tensor_tensor, nc.vector.tensor_reduce

            def over(v, n=4):
                return v.unsqueeze(2).to_broadcast([P, HALF, n])

            def first_best(hot, v, best, tmp, tmp1):
                own(TT(tmp, v, over(best), ALU.is_equal))
                own(TT(tmp, tmp, ramp.unsqueeze(1).to_broadcast([P, HALF, 4]), ALU.mult))
                own(TR(tmp1, tmp, AX.X, ALU.max))
                own(TT(hot, tmp, over(tmp1), ALU.is_equal))

            lg, le = rt[:, :, 40:44], rt[:, :, 44:60].rearrange("p h (g e) -> p h g e", g=NG)
            tmp, tmp1 = rt[:, :, 60:64], rt[:, :, 64]
            g_hot, e_sel, e_max, g_max = rt[:, :, 8:12], rt[:, :, 12:16], rt[:, :, 65], rt[:, :, 66]
            g_sum, p_group, e_sum = rt[:, :, 67], rt[:, :, 68], rt[:, :, 69]
            prob, rest, best = rt[:, :, 72:76], rt[:, :, 76:80], rt[:, :, 70]
            hot1, hot2, weight = rt[:, :, 80:84], rt[:, :, 84:88], rt[:, :, 88:92]
            wide4 = rt[:, :, 96:112].rearrange("p h (g e) -> p h g e", g=NG)

            dve.wait_ge(routed_pe, 1)
            own(TT(rt[:, :, 40:60], bank[0][:, 0:HALF * 20].rearrange("p (h n) -> p h n", h=HALF), rb[:, :, :],
                   ALU.add))
            own(TR(g_max, lg, AX.X, ALU.max))
            TT(rt[:, :, 0:4], lg, over(g_max), ALU.subtract).then_inc(small_dve, 1)
            first_best(g_hot, lg, g_max, tmp, tmp1)
            for h in range(HALF):
                own(TT(wide4[:, h], le[:, h], g_hot[:, h].unsqueeze(2).to_broadcast([P, NG, EG]), ALU.mult))
            for h in range(HALF):
                own(TR(e_sel[:, h], wide4[:, h].rearrange("p g e -> p e g"), AX.X, ALU.add))
            own(TR(e_max, e_sel, AX.X, ALU.max))
            TT(rt[:, :, 32:36], e_sel, over(e_max), ALU.subtract).then_inc(small_dve, 1)
            dve.wait_ge(small_act, 2)
            own(TR(g_sum, rt[:, :, 4:8], AX.X, ALU.add))
            own(nc.vector.reciprocal(p_group, g_sum))
            dve.wait_ge(small_act, 3)
            own(TR(e_sum, rt[:, :, 36:40], AX.X, ALU.add))
            own(nc.vector.reciprocal(e_sum, e_sum))
            own(TT(prob, rt[:, :, 36:40], over(e_sum), ALU.mult))
            own(TR(best, prob, AX.X, ALU.max))
            first_best(hot1, prob, best, tmp, tmp1)
            own(nc.vector.scalar_tensor_tensor(out=rest, in0=hot1, scalar=-2.0, in1=prob, op0=ALU.mult, op1=ALU.add))
            own(TR(best, rest, AX.X, ALU.max))
            first_best(hot2, rest, best, tmp, tmp1)
            own(TT(hot1, hot1, hot2, ALU.add))
            own(TT(weight, hot1, prob, ALU.mult))
            own(TR(tmp1, weight, AX.X, ALU.add))
            own(nc.vector.reciprocal(tmp1, tmp1))
            own(TT(weight, weight, over(tmp1), ALU.mult))
            own(TT(weight, weight, over(p_group), ALU.mult))
            for dst, chosen in ((mask, hot1), (comb, weight)):
                for h in range(HALF):
                    own(TT(dst[:, h, :].rearrange("p (g e) -> p g e", g=NG),
                           g_hot[:, h].unsqueeze(2).to_broadcast([P, NG, EG]),
                           chosen[:, h].unsqueeze(1).to_broadcast([P, NG, EG]), ALU.mult))
            nc.vector.tensor_copy(cmax[:, 0:1], ones[:, 0:1]).then_inc(small_dve, 1)
            dve.wait_ge(routed_pe, 2)
            ranks = bank[1][:, 0:HALF * NE].rearrange("p (h e) -> p h e", h=HALF)
            own(nc.vector.scalar_tensor_tensor(out=pos[:, :, :], in0=ranks, scalar=1.0, in1=mask[:, :, :],
                                               op0=ALU.add, op1=ALU.mult))
            own(nc.vector.tensor_scalar(pos[:, :, :], pos[:, :, :], -1.0, None, ALU.add))
            own(TR(cmax[:, 1:2], bank[1][:, 2 * NE:3 * NE], AX.X, ALU.max))
            own(nc.vector.tensor_scalar(cmax[:, 2:5], table[:, C_THR:C_THR + 3], cmax[:, 1:2], None, ALU.is_lt))
            own(TR(cmax[:, 5:6], cmax[:, 2:5], AX.X, ALU.add))
            nc.vector.tensor_scalar(n_pass[:, :], cmax[0:1, 5:6], 1.0, None, ALU.add).then_inc(pass_ready, 1)

            dve.wait_ge(pass_ready, 1)
            passes = dve.value_load(n_pass[0:1, 0:1], min_val=1, max_val=T // CAP)
            with dve.Fori(0, passes) as p:
                with dve.Fori(0, PAIRS) as i:
                    q = p * PAIRS + i
                    base = MOE0 + q * SLOTS_PAIR
                    dve.wait_ge(wt_full, FREE + q)
                    for half in range(HALF):
                        last = nc.vector.tensor_tensor(
                            pickD[:, half, :].rearrange("p (e s) -> p e s", e=2),
                            window.unsqueeze(1).to_broadcast([P, 2, CAP]),
                            pos[:, half, bass.ds(2 * i, 2)].unsqueeze(2).to_broadcast([P, 2, CAP]), ALU.is_equal)
                    last.then_inc(picks, 1)
                    dve.wait_ge(picks, 2 * q + 1)
                    for half in range(HALF):
                        last = nc.vector.tensor_tensor(
                            pickW[:, half, :].rearrange("p (e s) -> p e s", e=2),
                            pickD[:, half, :].rearrange("p (e s) -> p e s", e=2),
                            comb[:, half, bass.ds(2 * i, 2)].unsqueeze(2).to_broadcast([P, 2, CAP]), ALU.mult)
                    last.then_inc(picks, 1)
                    for c in range(4):
                        full, moved, n = ((b6_full, b6_moved, 7 * q), (b7_full, b7_moved, 6 * q))[c % 2]
                        dve.wait_ge(full, n + c // 2 + 1)
                        nc.vector.tensor_tensor(
                            xeT[:, 4 * c:4 * c + 4, :], bank[6 + c % 2][:, :].rearrange("p (k s) -> p k s", k=4),
                            gT[:, 2 * KD + 4 * c:2 * KD + 4 * c + 4].unsqueeze(2).to_broadcast([P, 4, P]),
                            ALU.mult).then_inc(moved, 1)
                    dve.wait_ge(wt_full, FREE + q + 1)
                    nc.vector.tensor_copy(pickWT[:, :], bank[2][:, 0:T]).then_inc(wt_moved, 1)
                    dve.wait_ge(gate_read, FREE + q + 1)
                    dve.wait_ge(slots_used, base + 16)
                    nc.vector.tensor_tensor(hid[:, :], sg[:, :], bank[1][:, :], ALU.mult).then_inc(hid_ready, 1)
                    dve.wait_ge(slots_used, base + SLOTS_PAIR)
                    for cb in range(2, 4):
                        nc.vector.tensor_copy(y_slots[:, cb * 512:(cb + 1) * 512],
                                              bank[2 + cb][:, :]).then_inc(y_moved_dve, 1)
                    for n in range(8):
                        cb, h = divmod(n, HALF)
                        full, moved, at = ((b7_full, b7_moved, 6 * q + 2), (b6_full, b6_moved, 7 * q + 3))[n % 2]
                        dve.wait_ge(full, at + n // 2 + 1)
                        part = x[:, h, cb * 512:(cb + 1) * 512]
                        nc.vector.tensor_tensor(part, part, bank[7 - n % 2][:, :], ALU.add).then_inc(moved, 1)
                nc.vector.tensor_scalar(window, window, float(CAP), None, ALU.add).then_inc(window_ready, 1)
                dve.wait_ge(window_ready, p + 1)

            dve.wait_ge(squares, HALF + 4 + 8 + HALF)
            rsqrt(4, HALF, 18, D)
            dve.wait_ge(gfin_loaded, 16)
            for h in range(HALF):
                nc.vector.scalar_tensor_tensor(out=wide[:, h, :], in0=x[:, h, :], scalar=rs[:, h:h + 1],
                                               in1=gfin[:, :], op0=ALU.mult, op1=ALU.mult).then_inc(out_ready, 1)

        @block.tensor
        def _(pe):
            def transposes(u):
                for b in range(ROUND):
                    for kk in range(PER_BANK):
                        for half in range(HALF):
                            k = PER_BANK * b + kk
                            last = nc.tensor.transpose(bank[b][:, kk * T + half * P:kk * T + (half + 1) * P],
                                                       wide[:, half, k * P:(k + 1) * P], ident)
                    last.then_inc(tr_full, 1)

            for s in (pv_full, wt_full):
                pe.sem_inc(s, FREE)
            pe.wait_ge(small_loaded, ALL_SMALL)
            nc.tensor.transpose(bank[7][:, 0:3 * KD], gains[:, :], ident[0:3 * KD, 0:3 * KD]).then_inc(small_pe, 1)
            nc.tensor.transpose(bank[7][0:BUCKETS + 1, 64:64 + HEADS], rel[:, :],
                                ident[0:HEADS, 0:HEADS]).then_inc(small_pe, 1)
            pe.wait_ge(small_dve, 2)
            nc.tensor.matmul(bank[7][0:HEADS, P:4 * P], relT[:, :], onehot[:, :], start=True,
                             stop=True).then_inc(small_pe, 1)
            pe.wait_ge(small_dve, 3)
            pe.wait_ge(scaled, 2)
            transposes(0)
            pe.wait_ge(tr_dve, 4)
            pe.wait_ge(tr_act, 4)
            for half in range(HALF):
                for k in range(KD):
                    last = nc.tensor.matmul(bank[6][:, half * FOX:(half + 1) * FOX], hT[:, k, half * P:(half + 1) * P],
                                            wf[:, k, :], start=(k == 0), stop=(k == KD - 1))
            last.then_inc(small_pe, 1)

            def gate_rows():
                pe.wait_ge(small_dve, 5)
                nc.tensor.matmul(bank[6][0:16, P:3 * P], lf[:, 0, :], tri_ones, start=True, stop=False)
                nc.tensor.matmul(bank[6][0:16, 2 * P:3 * P], lf[:, 1, :], tri, start=False,
                                 stop=True).then_inc(small_pe, 1)

            def step(h, qkv, attend):
                g = h - 1 if attend else None
                uses = bank7_uses(h) if attend else 0
                first = uses + 4 if attend else 0

                def scores(a):
                    if a == 0:
                        pe.wait_ge(t_moved, uses)
                        pe.wait_ge(gate_k_ready, h)
                        pe.wait_ge(small_dve, 6)
                    pe.wait_ge(s_moved, FREE + 4 * g + a)
                    for qt in range(HALF):
                        dst = bank[6][:, 0:P] if qt == 0 else bank[6][:, P:3 * P]
                        n = (qt + 1) * P
                        nc.tensor.matmul(dst, qT[:, a, qt * P:n], kT[:, a, 0:n], start=True, stop=False)
                        last = nc.tensor.matmul(dst, gate_q[:, qt * P:n], gate_k[:, a, 0:n], start=False, stop=True)
                    last.then_inc(s_full, 1)

                def turn(a):
                    pe.wait_ge(p_ready, FREE + 2 * (4 * g + a) + 2)
                    pe.wait_ge(t_moved, uses + a)
                    for n in range(3):
                        last = nc.tensor.transpose(bank[7][:, n * P:(n + 1) * P], pr[:, n * P:(n + 1) * P], ident)
                    last.then_inc(t_full, 1)

                def values(a):
                    pe.wait_ge(t_moved, uses + a + 1)
                    pe.wait_ge(v_moved, 2 * h)
                    if a >= 2:
                        pe.wait_ge(o_moved, 4 * g + a - 1)
                    dst, v = bank[4 + a % 2], v_tok[:, :, a * HD:(a + 1) * HD]
                    nc.tensor.matmul(dst[:, 0:HD], prT[:, 0:P], v[:, 0], start=True, stop=True)
                    nc.tensor.matmul(dst[:, HD:2 * HD], prT[:, P:2 * P], v[:, 0], start=True, stop=False)
                    nc.tensor.matmul(dst[:, HD:2 * HD], prT[:, 2 * P:3 * P], v[:, 1], start=False,
                                     stop=True).then_inc(pv_full, 1)

                def by_head(moved, n, part):
                    if part == 0:
                        pe.wait_ge(moved, 2 * h + 2)
                    pe.wait_ge(t_moved, first + n + part)
                    for a in range(2):
                        for half in range(HALF):
                            at = a * T + half * P
                            hd = (2 * part + a) * HD
                            last = nc.tensor.transpose(bank[7][:, at:at + P], qk_tok[:, half, hd:hd + HD], ident)
                    last.then_inc(t_full, 1)

                for s in range(SLOTS_QKV if qkv else 6):
                    if qkv:
                        b, j = divmod(s, KD // KPS)
                        if attend and j == 0:
                            pe.wait_ge((q_moved, k_moved, v_moved)[b], 2 * h)
                            if b == 2:
                                pe.wait_ge(o_moved, 4 * h)
                        pe.wait_ge(slot_in[s], 16 * (h + 1))
                        for k in range(KPS):
                            for half in range(HALF):
                                kd = j * KPS + k
                                last = nc.tensor.matmul(bank[2 * b + half][:, :], hT[:, kd, half * P:(half + 1) * P],
                                                        slot_block(s, k), start=(kd == 0), stop=(kd == KD - 1))
                        last.then_inc(slots_used, 1)
                        if not attend and s == 1:
                            gate_rows()
                    if attend:
                        if s < 4:
                            scores(s)
                        if 2 <= s < 6:
                            values(s - 2)
                        if 1 <= s < 5:
                            turn(s - 1)
                    if qkv and s in (5, 6):
                        by_head(q_moved, 0, s - 5)
                    if qkv and s in (9, 10):
                        by_head(k_moved, 2, s - 9)

            step(0, True, False)
            with pe.Fori(1, HEAD_GROUPS) as h:
                step(h, True, True)
            step(HEAD_GROUPS, False, True)

            pe.wait_ge(scaled, 2 + 4)
            transposes(1)
            pe.wait_ge(tr_dve, 8)
            pe.wait_ge(tr_act, 8)
            for i in range(SLOTS_OUT):
                n = SLOTS_IN + i
                cb, j = divmod(i, KD // KPS)
                pe.wait_ge(slot_in[n % RING], 16 * (n // RING + 1))
                for k in range(KPS):
                    for half in range(HALF):
                        kd = j * KPS + k
                        last = nc.tensor.matmul(bank[2 * cb + half][:, :], hT[:, kd, half * P:(half + 1) * P],
                                                slot_block(n % RING, k), start=(kd == 0), stop=(kd == KD - 1))
                last.then_inc(slots_used, 1)

            pe.wait_ge(scaled, 2 + 4 + 2)
            transposes(2)
            pe.wait_ge(tr_dve, 12)
            pe.wait_ge(tr_act, 12)
            for half in range(HALF):
                for k in range(KD):
                    last = nc.tensor.matmul(bank[0][:, half * 20:(half + 1) * 20], hT[:, k, half * P:(half + 1) * P],
                                            wr[:, k, :], start=(k == 0), stop=(k == KD - 1))
            last.then_inc(routed_pe, 1)
            pe.wait_ge(small_dve, 9)
            nc.tensor.matmul(bank[1][:, 0:NE], strict, mask[:, 0, :], start=True, stop=True)
            nc.tensor.matmul(bank[1][:, NE:2 * NE], ones, mask[:, 0, :], start=True, stop=False)
            nc.tensor.matmul(bank[1][:, NE:2 * NE], strict, mask[:, 1, :], start=False, stop=True)
            nc.tensor.matmul(bank[1][:, 2 * NE:3 * NE], ones, mask[:, 0, :], start=True, stop=False)
            nc.tensor.matmul(bank[1][:, 2 * NE:3 * NE], ones, mask[:, 1, :], start=False,
                             stop=True).then_inc(routed_pe, 1)

            pe.wait_ge(pass_ready, 1)
            passes = pe.value_load(n_pass[0:1, 0:1], min_val=1, max_val=T // CAP)
            with pe.Fori(0, passes) as p:
                with pe.Fori(0, PAIRS) as i:
                    q = p * PAIRS + i

                    def landed(j):
                        s, before = moe_slot(j)
                        pe.wait_ge(slot_in[s], 16 * (before + 1) + q * (16 * SLOTS_PAIR // RING))
                        return s

                    pe.wait_ge(picks, 2 * q + 1)
                    for c in range(4):
                        full, moved, n = ((b6_full, b6_moved, 7 * q), (b7_full, b7_moved, 6 * q))[c % 2]
                        pe.wait_ge(moved, FREE + n + c // 2)
                        for k in range(4):
                            for half in range(HALF):
                                kd = 4 * c + k
                                last = nc.tensor.matmul(bank[6 + c % 2][:, k * P:(k + 1) * P],
                                                        wide[:, half, kd * P:(kd + 1) * P], pickD[:, half, :],
                                                        start=(half == 0), stop=(half == HALF - 1))
                        last.then_inc(full, 1)
                    pe.wait_ge(picks, 2 * q + 2)
                    pe.wait_ge(y_moved_act, FREE + 2 * q)
                    for half in range(HALF):
                        last = nc.tensor.transpose(bank[2][:, half * P:(half + 1) * P], pickW[:, half, :], ident)
                    last.then_inc(wt_full, 1)

                    pe.wait_ge(b6_moved, FREE + 7 * q + 2)
                    pe.wait_ge(b7_moved, FREE + 6 * q + 2)
                    pe.wait_ge(gate_read, FREE + q)
                    pe.wait_ge(hid_ready, FREE + q)
                    for m in range(2):
                        for j in range(KD // KPS):
                            at = 2 * (m * (KD // KPS) + j)
                            s = [landed(at + e) for e in range(2)]
                            for k in range(KPS):
                                kd = KPS * j + k
                                for e in range(2):
                                    last = nc.tensor.matmul(bank[m][e * CAP:(e + 1) * CAP, :],
                                                            xeT[:, kd, e * CAP:(e + 1) * CAP], slot_block(s[e], k),
                                                            start=(kd == 0), stop=(kd == KD - 1))
                                    if k == KPS - 1:
                                        last.then_inc(slots_used, 1)

                    pe.wait_ge(hid_ready, FREE + q + 1)
                    for k in range(KF):
                        last = nc.tensor.transpose(bank[6][:, k * P:(k + 1) * P], hid[:, k * P:(k + 1) * P], ident)
                    last.then_inc(b6_full, 1)
                    pe.wait_ge(b6_moved, FREE + 7 * q + 3)
                    pe.wait_ge(wt_moved, q + 1)
                    pe.wait_ge(y_moved_dve, FREE + 2 * q)
                    for k in range(KF):
                        s = [landed(2 * (2 * KD // KPS + k) + e) for e in range(2)]
                        for cb in range(4):
                            for e in range(2):
                                last = nc.tensor.matmul(bank[2 + cb][e * CAP:(e + 1) * CAP, :],
                                                        hidT[:, k, e * CAP:(e + 1) * CAP], slot_block(s[e], cb),
                                                        start=(k == 0), stop=(k == KF - 1))
                                if cb == 3:
                                    last.then_inc(slots_used, 1)
                    for n in range(8):
                        cb, half = divmod(n, HALF)
                        full, moved, at = ((b7_full, b7_moved, 6 * q + 2), (b6_full, b6_moved, 7 * q + 3))[n % 2]
                        if half == 0:
                            pe.wait_ge(y_moved_act if cb < 2 else y_moved_dve, FREE + 2 * q + cb % 2 + 1)
                        pe.wait_ge(moved, FREE + at + n // 2)
                        nc.tensor.matmul(bank[7 - n % 2][:, :], pickWT[:, half * P:(half + 1) * P],
                                         y_slots[:, cb * 512:(cb + 1) * 512], start=True, stop=True).then_inc(full, 1)


_INS = ["x", "attn_norm_g", "w_in", "b_forget", "fox_out_norm_g", "moba_out_norm_g", "rel_bias", "w_out", "ffn_norm_g",
        "w_group_router", "b_group_router", "w_expert_router", "b_expert_router", "w_gate", "w_up", "w_down",
        "final_norm_g"]
_OUT = (1, T, D)


def kernel(**inputs):
    import concourse.bacc as bacc
    from concourse.bass_utils import run_bass_kernel_spmd

    nc = bacc.Bacc("TRN2", target_bir_lowering=False, num_devices=1)
    arrays = {n: np.ascontiguousarray(inputs[n]) for n in _INS}
    arrays |= dict(zip(("table", "onehot", "pick", "frame"), constants()))
    args = [nc.dram_tensor(f"in_{n}", a.shape, mybir.dt.from_np(a.dtype), kind="ExternalInput").ap()
            for n, a in arrays.items()]
    args.append(nc.dram_tensor("out", _OUT, F32, kind="ExternalOutput").ap())
    layer(nc, *args)
    r = run_bass_kernel_spmd(nc, [{f"in_{n}": a for n, a in arrays.items()}], core_ids=[0])
    return r.results[0]["out"]
```

```python
from contextlib import ExitStack

import numpy as np

import concourse.bass as bass
from concourse import mybir

ALU = mybir.AluOpType
ACT = mybir.ActivationFunctionType
AX = mybir.AxisListType
F32 = mybir.dt.float32
F32R = mybir.dt.float32r
I32 = mybir.dt.int32

P = 128
T = 256
HALF = T // P
D = 2048
KD = D // P
HD = 128
HEADS = 16
FOX = 8
GROUP_H = 4
HEAD_GROUPS = HEADS // GROUP_H
NE = 16
F = 512
KF = F // P
CAP = 64
PAIRS = NE // 2
NG = 4
EG = NE // NG
EPS = 1e-6
NEG = -1e30
BUCKETS = 32
SCALE = HD ** -0.5

SLOT = 2048
RING = 6
MOE_RING = 12
KPS = SLOT // 512
FREE = 1

SLOTS_QKV = 3 * KD // KPS
SLOTS_IN = HEAD_GROUPS * SLOTS_QKV
SLOTS_OUT = (D // 512) * KD // KPS
SLOTS_PAIR = 2 * (2 * KD // KPS + KF * D // SLOT)
SLOTS_PASS = PAIRS * SLOTS_PAIR
N_HALVES = 2 * (SLOTS_IN + SLOTS_OUT)
SPLITS = 4
HALF_SLOT = SLOT // 2
assert SLOTS_QKV % RING == 0 and SLOTS_PAIR % MOE_RING == 0

COLS, C_N = {}, 0
for _name, _n in (("ident", P), ("tri", P), ("ones", P), ("strict", P), ("window", CAP), ("ramp", 4), ("steps", 4),
                  ("gT", 3 * KD), ("wf", KD * FOX + 88), ("wr", KD * (NG + NE) + 76), ("bf", HALF * FOX),
                  ("rb", HALF * (NG + NE)), ("relT", HEADS), ("onehot", 384), ("pick", 2 + 2 * HEADS)):
    COLS[_name] = slice(C_N, C_N + _n)
    C_N += _n
NARROW = 96


def small_table(i):
    r = np.arange(P)
    table = np.zeros((P, C_N), np.float32)

    def put(name, a):
        a = np.asarray(a).reshape(len(a), -1)
        table[:a.shape[0], COLS[name].start:COLS[name].start + a.shape[1]] = a

    put("ident", np.eye(P))
    put("tri", r[:, None] <= r[None, :])
    put("ones", np.ones((P, P)))
    put("strict", r[:, None] < r[None, :])
    put("window", np.tile(np.arange(CAP), (P, 1)))
    put("ramp", np.tile([4, 3, 2, 1], (P, 1)))
    put("steps", np.tile([CAP, 2 * CAP, 3 * CAP], (P, 1)))
    gains = np.concatenate([i[n].reshape(-1) for n in ("attn_norm_g", "fox_out_norm_g", "moba_out_norm_g",
                                                       "ffn_norm_g")])
    put("gT", gains.reshape(3 * KD, P).T)
    put("wf", i["w_in"][0, :, 3 * D:].reshape(KD, P, FOX).transpose(1, 0, 2))
    routers = np.concatenate([i["w_group_router"][0], i["w_expert_router"][0].reshape(D, NE)], 1)
    put("wr", routers.reshape(KD, P, NG + NE).transpose(1, 0, 2))
    put("bf", np.tile(i["b_forget"], (P, HALF)))
    put("rb", np.tile(np.concatenate([i["b_group_router"].reshape(-1), i["b_expert_router"].reshape(-1)]), (P, HALF)))
    relT = np.zeros((BUCKETS + 1, HEADS), np.float32)
    relT[:BUCKETS, FOX:] = i["rel_bias"].T
    relT[BUCKETS] = 1.0
    put("relT", relT)
    dist = np.arange(-(P - 1), T)
    d = np.maximum(dist, 0)
    exact = BUCKETS // 2
    ratio = np.log(np.maximum(d, 1).astype(np.float32) / exact) / np.log(128 / exact)
    large = np.minimum(exact + (ratio * (BUCKETS - exact)).astype(np.int32), BUCKETS - 1)
    bucket = np.where(d < exact, d, large)
    onehot = np.zeros((BUCKETS + 1, 384), np.float32)
    onehot[bucket[dist >= 0], np.nonzero(dist >= 0)[0]] = 1.0
    onehot[BUCKETS, :dist.size][dist < 0] = NEG
    put("onehot", onehot)
    rows = np.arange(16)
    pick = np.zeros((16, 2 + 2 * HEADS), np.float32)
    pick[:, 0] = rows < FOX
    pick[:, 1] = rows >= FOX
    for h in range(FOX):
        pick[:, 2 + h] = rows == FOX + h
        pick[:, 2 + HEADS + h] = rows == h
    put("pick", pick)
    return table


def layer(nc, x_in, xT_in, small_in, w_in, w_out, w_gate, w_up, w_down, g_final, out):
    ctx = ExitStack()
    with ctx:
        def sem(name):
            return ctx.enter_context(nc.semaphore(name))

        start, attention = ExitStack(), ExitStack()

        def sb(name, shape, dt=F32, until=ctx):
            return until.enter_context(nc.sbuf_tensor(name, shape, dt))

        sb("before_xT", [P, SPLITS * HALF_SLOT * 2 + KD * T], F32, start)
        xT = sb("xT", [P, KD, T], F32, start)
        start.close()
        w_hi = sb("w_hi", [P, SPLITS, HALF_SLOT], F32R, attention)
        w_lo = sb("w_lo", [P, SPLITS, HALF_SLOT], F32R, attention)
        oT_lo = sb("oT_lo", [P, KD, T], F32R, attention)
        oT_hi = sb("oT_hi", [P, KD, T], F32R, attention)
        hT_hi = sb("hT_hi", [P, KD, T], F32R, attention)
        hT_lo = sb("hT_lo", [P, KD, T], F32R, attention)
        attention.close()
        extra = sb("extra", [P, 6, SLOT])
        y_sum = sb("y_sum", [P, HALF, D])
        gfin = sb("gfin", [P, D])
        sg = sb("sg", [P, F])
        hid = sb("hid", [P, F])
        hidT = sb("hidT", [P, KF, P])
        pickD = sb("pickD", [P, HALF, 2 * CAP])
        pickW = sb("pickW", [P, HALF, 2 * CAP])
        pickWT = sb("pickWT", [P, T])
        sb("rest_of_hT", [P, 2 * KD * T - D - 3 * F - 3 * T])

        ring = sb("ring", [P, RING, SLOT])
        x = sb("x", [P, HALF, D])
        heads = sb("heads", [P, 2048])
        qT = heads[:, 0:1024].rearrange("p (a t) -> p a t", a=GROUP_H)
        kT = heads[:, 1024:2048].rearrange("p (a t) -> p a t", a=GROUP_H)
        xeT = heads[:, :].rearrange("p (k s) -> p k s", k=KD)
        rows = sb("rows", [P, 2048])
        qk_tok = rows[:, 0:1024].rearrange("p (h n) -> p h n", h=HALF)
        v_tok = rows[:, 1024:2048].rearrange("p (h n) -> p h n", h=HALF)
        y_slots = rows[:, :]
        small = sb("small", [P, C_N])

        def of(name, rows_=P):
            return small[0:rows_, COLS[name]]

        ident, tri, ones, strict = of("ident"), of("tri"), of("ones"), of("strict")
        tri_ones = small[:, COLS["tri"].start:COLS["ones"].stop]
        window, ramp, gT, pick = of("window"), of("ramp"), of("gT"), of("pick", 16)
        n_wf, n_wr = (COLS[n].stop - COLS[n].start for n in ("wf", "wr"))
        wf_hi, wf_lo = sb("wf_hi", [P, n_wf], F32R), sb("wf_lo", [P, n_wf], F32R)
        wr_hi, wr_lo = sb("wr_hi", [P, n_wr], F32R), sb("wr_lo", [P, n_wr], F32R)
        band_dram = nc.dram_tensor("band_dram", [HEADS, 384], F32)
        bias = sb("bias", [P, GROUP_H, T])
        crow = sb("crow", [16, T])
        gate_q = sb("gate_q", [16, T])
        gate_k = sb("gate_k", [16, GROUP_H, T])
        lf = sb("lf", [P, HALF, 16])
        zf = sb("zf", [P, 4, 16])
        sc = sb("sc", [P, 384])
        pr = sb("pr", [P, 384])
        prT = sb("prT", [P, 384])
        band = sc[0:HEADS, :]
        nmx = sb("nmx", [P, 2])
        rsum = sb("rsum", [P, 2])
        rinv = sb("rinv", [P, 2])
        sq = sb("sq", [P, T])
        sqs = sb("sqs", [P, 2, T])
        ssq = sb("ssq", [P, 16])
        ms = sb("ms", [P, 2])
        lnms = sb("lnms", [P, 2])
        r0 = sb("r0", [P, 2])
        r1 = sb("r1", [P, 2])
        rs = sb("rs", [P, 5, 2])
        rsq = sb("rsq", [P, 2])
        rt = sb("rt", [P, HALF, 112])
        mask = sb("mask", [P, HALF, NE])
        comb = sb("comb", [P, HALF, NE])
        pos = sb("pos", [P, HALF, NE])
        cmax = sb("cmax", [P, 8])
        n_pass = sb("n_pass", [1, 1], I32)

        bank = [ctx.enter_context(nc.psum_tensor(f"bank{i}", [P, 512], F32)) for i in range(8)]

        xT_in_s = [sem(f"xT_loaded{c}") for c in range(4)]
        x_loaded, small_loaded, gfin_loaded = sem("x_loaded"), sem("small_loaded"), sem("gfin_loaded")
        slot_in = [sem(f"slot_in{s}") for s in range(RING)]
        halves_hi, halves_split = sem("halves_hi"), sem("halves_split")
        halves_used = sem("halves_used")
        moe_in = [sem(f"moe_in{s}") for s in range(MOE_RING)]
        moe_used = sem("moe_used")
        hT_hi_ready, hT_ready = sem("hT_hi_ready"), sem("hT_ready")
        wsmall_hi, wsmall_ready = sem("wsmall_hi"), sem("wsmall_ready")
        band_stored, bias_loaded = sem("band_stored"), sem("bias_loaded")
        squares = sem("squares")
        ms_ready, r0_ready, rs_ready = sem("ms_ready"), sem("r0_ready"), sem("rs_ready")
        small_pe, small_dve, small_act = sem("small_pe"), sem("small_dve"), sem("small_act")
        q_moved, k_moved, v_moved = sem("q_moved"), sem("k_moved"), sem("v_moved")
        t_full, t_moved = sem("t_full"), sem("t_moved")
        s_full, s_moved = sem("s_full"), sem("s_moved")
        nmx_ready, exps_ready, pr_ready = sem("nmx_ready"), sem("exps_ready"), sem("pr_ready")
        pv_full, o_hi_ready, o_moved = sem("pv_full"), sem("o_hi_ready"), sem("o_moved")
        sq_added = sem("sq_added")
        gate_k_ready = sem("gate_k_ready")
        sums_full = sem("sums_full")
        sums_read = sem("sums_read")
        fox_added = sem("fox_added")
        x_added = sem("x_added")
        xt_full, xt_hi, xt_moved = sem("xt_full"), sem("xt_hi"), sem("xt_moved")
        routed_pe, pass_ready = sem("routed_pe"), sem("pass_ready")
        y_begun = sem("y_begun")
        picks = sem("picks")
        b6_full, b6_moved, b7_full, b7_moved = sem("b6_full"), sem("b6_moved"), sem("b7_full"), sem("b7_moved")
        wt_full, wt_moved = sem("wt_full"), sem("wt_moved")
        gate_read, hid_ready = sem("gate_read"), sem("hid_ready")
        y_moved_act, y_moved_dve = sem("y_moved_act"), sem("y_moved_dve")
        out_ready, out_stored = sem("out_ready"), sem("out_stored")
        window_ready = sem("window_ready")
        dve_step, act_step = sem("dve_step"), sem("act_step")

        block = ctx.enter_context(nc.Block())

        w_in_v = w_in.rearrange("o (j k p) n -> (o p) j k n", p=P, k=KPS)
        w_out_v = w_out.rearrange("o (j k p) n -> (o p) j k n", p=P, k=KPS)
        w_gate_v = w_gate.rearrange("o e (j k p) f -> p (o e) j k f", p=P, k=KPS)
        w_up_v = w_up.rearrange("o e (j k p) f -> p (o e) j k f", p=P, k=KPS)
        w_down_v = w_down.rearrange("o e (k p) d -> p (o e) k d", p=P)
        gT_cols = COLS["gT"].start

        OUT_ORDER = [(kind, cb, 2 * kind + j) for kind in range(2) for cb in range(4) for j in range(2)]
        XT_BANK = {0: 4, 1: 6, 2: 0, 3: 2}
        OUT_BANKS = {(0, 0): 0, (0, 1): 2, (0, 2): 0, (0, 3): 2, (1, 0): 4, (1, 1): 6, (1, 2): 0, (1, 3): 2}

        def moe_slot(j):
            s = j % MOE_RING
            return ring[:, (SLOTS_IN + SLOTS_OUT + s) % RING, :] if s < RING else extra[:, s - RING, :]

        def tokens_of(cols):
            return cols.rearrange("p (k t) -> p k t", k=2)

        def bank7_uses(h):
            return 8 * h - 4

        class Own:

            def __init__(self, eng, own):
                self.eng, self.own, self.n = eng, own, 0

            def __call__(self, ins):
                self.n += 1
                ins.then_inc(self.own, 1)
                self.eng.wait_ge(self.own, self.n)

        def half_block(n):
            s, part = divmod(n, 2)
            return s, s % RING, slice(part * HALF_SLOT, (part + 1) * HALF_SLOT)

        @block.sync
        def _(sp):
            def qkv_load(hg, s, first):
                b, j = divmod(s, KD // KPS)
                kind, half = divmod(hg, 2) if first else (hg // 2, hg % 2)
                col = kind * 3072 + half * 512 + b * 1024
                if not first or s >= RING:
                    sp.wait_ge(halves_split, 2 * (hg * SLOTS_QKV + s - RING + 1))
                sp.dma_start(ring[:, s % RING, :].rearrange("p (k n) -> p k n", k=KPS),
                             w_in_v[:, j, :, bass.ds(col, 512)]).then_inc(slot_in[s % RING], 16)

            for c in range(4):
                sp.dma_start(xT[:, 4 * c:4 * c + 4, :], xT_in[:, 4 * c:4 * c + 4, :]).then_inc(xT_in_s[c], 16)
                if c == 0:
                    sp.dma_start(small[:, :], small_in).then_inc(small_loaded, 16)
                if c < 3:
                    qkv_load(0, c, True)
            for h in range(HALF):
                sp.dma_start(x[:, h, :], x_in[0, h * P:(h + 1) * P, :]).then_inc(x_loaded, 16)
            for s in range(3, SLOTS_QKV):
                qkv_load(0, s, True)
            with sp.Fori(1, HEAD_GROUPS) as hg:
                for s in range(SLOTS_QKV):
                    qkv_load(hg, s, False)
            for i, (_, cb, j) in enumerate(OUT_ORDER):
                n = SLOTS_IN + i
                sp.wait_ge(halves_split, 2 * (n - RING + 1))
                sp.dma_start(ring[:, n % RING, :].rearrange("p (k n) -> p k n", k=KPS),
                             w_out_v[:, j, :, cb * 512:(cb + 1) * 512]).then_inc(slot_in[n % RING], 16)

            def pair_loads(base, pair, first=False):
                j = 0
                for w, n in ((w_gate_v, KD // KPS), (w_up_v, KD // KPS), (w_down_v, KF)):
                    for c in range(n):
                        for e in range(2):
                            if not first or j >= MOE_RING:
                                sp.wait_ge(moe_used, base + (j - MOE_RING + 1))
                            elif j < RING:
                                sp.wait_ge(halves_split, 2 * (SLOTS_IN + SLOTS_OUT - RING + 1 + j))
                            else:
                                sp.wait_ge(halves_used, N_HALVES)
                            src = w[:, bass.ds(2 * pair + e, 1), c]
                            dst = moe_slot(j)
                            if w is w_down_v:
                                src = src.rearrange("p o d -> p (o d)")
                            else:
                                dst, src = dst.rearrange("p (k f) -> p k f", k=KPS), src.rearrange("p o k f -> p (o k) f")
                            sp.dma_start(dst, src).then_inc(moe_in[j % MOE_RING], 16)
                            j += 1

            pair_loads(0, 0, True)
            with sp.Fori(1, PAIRS) as pair:
                pair_loads(pair * SLOTS_PAIR, pair)
            sp.wait_ge(pass_ready, 1)
            passes = sp.value_load(n_pass[0:1, 0:1], min_val=1, max_val=T // CAP)
            with sp.If(passes > 1):
                with sp.Fori(1, passes) as p:
                    with sp.Fori(0, PAIRS) as pair:
                        pair_loads(p * SLOTS_PASS + pair * SLOTS_PAIR, pair)
            for h in range(HALF):
                sp.wait_ge(out_ready, h + 1)
                sp.dma_start(out[0, h * P:(h + 1) * P, :], x[:, h, :]).then_inc(out_stored, 16)
            sp.wait_ge(out_stored, 16 * HALF)

        @block.scalar
        def _(act):
            own = Own(act, act_step)
            for s in (exps_ready, gate_read, y_moved_act):
                act.sem_inc(s, FREE)

            def rsqrt_start(k):
                act.wait_ge(ms_ready, k)
                own(nc.scalar.activation(lnms[:, :], ms[:, :], ACT.Ln))
                nc.scalar.activation(r0[:, :], lnms[:, :], ACT.Exp, scale=-0.5).then_inc(r0_ready, 1)

            def high(h, n):
                s, at, cols = half_block(n)
                done = 2 * SLOTS_QKV * h + n
                act.wait_ge(slot_in[at], 16 * (SLOTS_QKV // RING * h + s // RING + 1))
                if not (isinstance(h, int) and done < SPLITS):
                    act.wait_ge(halves_used, done - SPLITS + 1)
                nc.scalar.activation(w_hi[:, n % SPLITS, :], ring[:, at, cols], ACT.Copy).then_inc(halves_hi, 1)

            act.wait_ge(small_loaded, 16)
            for k in range(KD):
                if k % 4 == 0:
                    act.wait_ge(xT_in_s[k // 4], 16)
                nc.scalar.activation(hT_hi[:, k, :], xT[:, k, :], ACT.Copy,
                                     scale=gT[:, k:k + 1]).then_inc(hT_hi_ready, 1)
                if k == 3:
                    high(0, 0)
                if k == 7:
                    high(0, 1)
            high(0, 2)
            nc.scalar.activation(wf_hi[:, :], of("wf"), ACT.Copy).then_inc(wsmall_hi, 1)
            high(0, 3)
            nc.scalar.activation(wr_hi[:, :], of("wr"), ACT.Copy).then_inc(wsmall_hi, 1)

            def attend(h, s):
                g = h - 1

                def turned(a):
                    act.wait_ge(t_full, bank7_uses(h) + a + 1)
                    act.wait_ge(pv_full, FREE + 4 * g + a)
                    nc.scalar.activation(prT[:, :], bank[7][:, 0:3 * P], ACT.Copy).then_inc(t_moved, 1)

                def exps(a):
                    act.wait_ge(nmx_ready, 4 * g + a + 1)
                    act.wait_ge(t_full, bank7_uses(h) + a)
                    for qt, (lo, hi) in enumerate(((0, P), (P, 3 * P))):
                        last = nc.scalar.activation(pr[:, lo:hi], sc[:, lo:hi], ACT.Exp, bias=nmx[:, qt:qt + 1],
                                                    accum_out=rsum[:, qt:qt + 1])
                    last.then_inc(exps_ready, 1)

                def outputs(a):
                    n = 4 * g + a
                    act.wait_ge(pv_full, FREE + n + 1)
                    act.wait_ge(sq_added, 1 + n)
                    src = bank[4 + a % 2][:, 0:T]
                    nc.scalar.activation(oT_hi[:, bass.ds(n, 1), :].rearrange("p o t -> p (o t)"), src, ACT.Copy,
                                         scale=small[:, bass.ds(gT_cols + KD + n, 1)])
                    nc.scalar.activation(sq[:, :], src, ACT.Square).then_inc(o_hi_ready, 1)

                if 1 <= s <= 4:
                    turned(s - 1)
                if s < 4:
                    exps(s)
                if 2 <= s < 6:
                    outputs(s - 2)

            def period(h, s, attending):
                high(h, 2 * s + 4)
                if attending:
                    attend(h, s)
                high(h, 2 * s + 5)
                if s in (3, 7, 11):
                    b = s // 4
                    act.wait_ge(halves_used, 2 * SLOTS_QKV * h + 2 * s + 2)
                    if b < 2 and (attending or b):
                        act.wait_ge(t_full, (bank7_uses(h) if attending else 0) + (4 if attending else 0) * b
                                    + (2 if b else 0))
                    dst, moved = ((qk_tok, q_moved), (qk_tok, k_moved), (v_tok, v_moved))[b]
                    for half in range(HALF):
                        scale = (rsq if b == 0 else rs[:, 0])[:, half:half + 1]
                        nc.scalar.activation(dst[:, half, :], bank[2 * b + half][:, :], ACT.Copy,
                                             scale=scale).then_inc(moved, 1)

            for s in range(SLOTS_QKV):
                if s == 2:
                    act.wait_ge(x_loaded, 16 * HALF)
                    for h in range(HALF):
                        nc.scalar.activation((heads, rows)[h][:, :], x[:, h, :], ACT.Square,
                                             accum_out=ssq[:, h:h + 1]).then_inc(squares, 1)
                    rsqrt_start(1)
                if s == 3:
                    act.wait_ge(rs_ready, 1)
                period(0, s, False)
                if s == 5:
                    act.wait_ge(small_dve, 2)
                    own(nc.scalar.activation(zf[:, 3, :], zf[:, 2, :], ACT.Exp, scale=-1.0))
                    nc.scalar.activation(zf[:, 2, :], zf[:, 3, :], ACT.Ln, bias=1.0).then_inc(small_act, 1)
            with act.Fori(1, HEAD_GROUPS) as h:
                for s in range(SLOTS_QKV):
                    period(h, s, True)

            def new_x(cb):
                for h in range(HALF):
                    act.wait_ge(x_added, 2 * cb + h + 1)
                    part = slice(cb * 512, (cb + 1) * 512)
                    nc.scalar.activation((heads, rows)[h][:, part], x[:, h, part], ACT.Square,
                                         accum_out=ssq[:, 2 + 4 * h + cb:3 + 4 * h + cb]).then_inc(squares, 1)

            def new_xT(cb):
                for k in range(4 * cb, 4 * cb + 4):
                    if k % 2 == 0:
                        act.wait_ge(xt_full, k // 2 + 1)
                    nc.scalar.activation(hT_hi[:, k, :], bank[XT_BANK[cb] + k % 4 // 2][:, k % 2 * T:(k % 2 + 1) * T],
                                         ACT.Copy, scale=gT[:, 2 * KD + k:2 * KD + k + 1]).then_inc(xt_hi, 1)

            for i in range(SLOTS_OUT):
                if 2 * i + 4 < 2 * SLOTS_OUT:
                    high(HEAD_GROUPS, 2 * i + 4)
                if i < 6:
                    attend(HEAD_GROUPS, i)
                if 2 * i + 5 < 2 * SLOTS_OUT:
                    high(HEAD_GROUPS, 2 * i + 5)
                if i == 1:
                    rsqrt_start(2)
                if i == 8:
                    rsqrt_start(3)
                if i in (10, 12, 14):
                    new_x(i // 2 - 5)
                if i in (12, 14):
                    new_xT(i // 2 - 6)
            new_x(3)
            new_xT(2)
            rsqrt_start(4)
            new_xT(3)
            act.wait_ge(small_dve, 5)
            nc.scalar.activation(rt[:, :, 4:8], rt[:, :, 0:4], ACT.Exp).then_inc(small_act, 1)
            act.wait_ge(small_dve, 6)
            nc.scalar.activation(rt[:, :, 36:40], rt[:, :, 32:36], ACT.Exp).then_inc(small_act, 1)

            act.wait_ge(pass_ready, 1)
            act.dma_start(gfin[:, :], g_final.partition_broadcast(P)).then_inc(gfin_loaded, 16)
            for h in range(HALF):
                nc.scalar.activation(y_sum[:, h, :], x[:, h, :], ACT.Copy).then_inc(y_begun, 1)
            passes = act.value_load(n_pass[0:1, 0:1], min_val=1, max_val=T // CAP)
            with act.Fori(0, passes) as p:
                with act.Fori(0, PAIRS) as i:
                    q = p * PAIRS + i
                    base = q * SLOTS_PAIR
                    act.wait_ge(moe_used, base + 8)
                    act.wait_ge(hid_ready, FREE + q)
                    nc.scalar.activation(sg[:, :], bank[0][:, :], ACT.Silu).then_inc(gate_read, 1)
                    act.wait_ge(b6_full, 7 * q + 3)
                    nc.scalar.activation(hidT[:, :, :].rearrange("p k s -> p (k s)"), bank[6][:, :],
                                         ACT.Copy).then_inc(b6_moved, 1)
                    act.wait_ge(moe_used, base + SLOTS_PAIR)
                    for cb in range(2):
                        nc.scalar.activation(y_slots[:, cb * 512:(cb + 1) * 512], bank[2 + cb][:, :],
                                             ACT.Copy).then_inc(y_moved_act, 1)

            act.wait_ge(b6_moved, FREE + passes * (7 * PAIRS))
            act.wait_ge(b7_moved, FREE + passes * (6 * PAIRS))
            for h in range(HALF):
                nc.scalar.activation(x[:, h, :], y_sum[:, h, :], ACT.Square,
                                     accum_out=ssq[:, 12 + h:13 + h]).then_inc(squares, 1)
            rsqrt_start(5)

        @block.gpsimd
        def _(pool):
            nc.gpsimd.memset(sqs[:, :, :], 0.0).then_inc(sq_added, 1)
            pool.wait_ge(small_dve, 1)
            pool.dma_start(band_dram.ap(), band).then_inc(band_stored, 16)
            pool.wait_ge(band_stored, 16)
            windows = bass.AP(tensor=band_dram, offset=0, ap=[[1, P], [384, HEADS], [1, T]])
            pool.dma_start(bias[:, :, :], windows[:, 0:GROUP_H, :]).then_inc(bias_loaded, 16)

            for n in range(HEADS):
                g, a = divmod(n, GROUP_H)
                if g < HEAD_GROUPS - 1 and a == 0:
                    pool.wait_ge(s_moved, FREE + 4 * g + 4)
                    pool.dma_start(bias[:, :, :], windows[:, GROUP_H * (g + 1):GROUP_H * (g + 2), :]).then_inc(
                        bias_loaded, 16)
                pool.wait_ge(o_hi_ready, n + 1)
                pool.wait_ge(sq_added, 1 + n)
                dst = sqs[:, n // FOX, :]
                nc.gpsimd.tensor_tensor(dst, dst, sq[:, :], ALU.add).then_inc(sq_added, 1)

        @block.vector
        def _(dve):
            own = Own(dve, dve_step)
            for s in (s_moved, b6_moved, b7_moved, y_moved_dve, hid_ready, pr_ready, o_moved):
                dve.sem_inc(s, FREE)

            def rsqrt(k, sums, width):
                nc.vector.tensor_scalar(ms[:, :], sums, 1.0 / width, EPS, ALU.mult, ALU.add).then_inc(ms_ready, 1)
                dve.wait_ge(ms_ready, k)
                dve.wait_ge(r0_ready, k)
                own(nc.vector.tensor_tensor(r1[:, :], r0[:, :], r0[:, :], ALU.mult))
                own(nc.vector.tensor_tensor(r1[:, :], r1[:, :], ms[:, :], ALU.mult))
                own(nc.vector.tensor_scalar(r1[:, :], r1[:, :], -0.5, 1.5, ALU.mult, ALU.add))
                own(nc.vector.tensor_tensor(rs[:, k - 1, :], r0[:, :], r1[:, :], ALU.mult))

            def low(h, n):
                s, at, cols = half_block(n)
                done = 2 * SLOTS_QKV * h + n
                dve.wait_ge(halves_hi, done + 1)
                ins = nc.vector.tensor_tensor(w_lo[:, n % SPLITS, :], ring[:, at, cols],
                                              w_hi[:, n % SPLITS, :].bitcast(F32), ALU.subtract)
                ins.then_inc(halves_split, 1)

            dve.wait_ge(small_pe, 1)
            nc.vector.tensor_copy(band, bank[7][0:HEADS, 0:384]).then_inc(small_dve, 1)
            for k in range(KD):
                dve.wait_ge(hT_hi_ready, k + 1)
                nc.vector.scalar_tensor_tensor(out=hT_lo[:, k, :], in0=xT[:, k, :], scalar=gT[:, k:k + 1],
                                               in1=hT_hi[:, k, :].bitcast(F32), op0=ALU.mult,
                                               op1=ALU.subtract).then_inc(hT_ready, 1)
                if k == 3:
                    low(0, 0)
                if k == 7:
                    low(0, 1)
            low(0, 2)
            dve.wait_ge(wsmall_hi, 1)
            nc.vector.tensor_tensor(wf_lo[:, :], of("wf"), wf_hi[:, :].bitcast(F32),
                                    ALU.subtract).then_inc(wsmall_ready, 1)
            low(0, 3)
            dve.wait_ge(wsmall_hi, 2)
            nc.vector.tensor_tensor(wr_lo[:, :], of("wr"), wr_hi[:, :].bitcast(F32),
                                    ALU.subtract).then_inc(wsmall_ready, 1)

            def attend(h, s, part):
                g = h - 1

                def scores(a):
                    dve.wait_ge(s_full, 4 * g + a + 1)
                    if a == 0:
                        dve.wait_ge(bias_loaded, 16 * (g + 1))
                    dve.wait_ge(exps_ready, FREE + 4 * g + a)
                    for qt, (lo, hi) in enumerate(((0, P), (P, 3 * P))):
                        last = nc.vector.tensor_tensor(sc[:, lo:hi], bank[6][:, lo:hi],
                                                       bias[:, a, 0:hi - lo][:, ::-1], ALU.add)
                    last.then_inc(s_moved, 1)
                    dve.wait_ge(s_moved, FREE + 4 * g + a + 1)
                    for qt, (lo, hi) in enumerate(((0, P), (P, 3 * P))):
                        last = nc.vector.tensor_reduce(nmx[:, qt:qt + 1], sc[:, lo:hi], AX.X, ALU.max, negate=True)
                    last.then_inc(nmx_ready, 1)

                def probs(a):
                    dve.wait_ge(exps_ready, FREE + 4 * g + a + 1)
                    nc.vector.reciprocal(rinv[:, :], rsum[:, :]).then_inc(pr_ready, 1)
                    dve.wait_ge(pr_ready, FREE + 2 * (4 * g + a) + 1)
                    for qt, (lo, hi) in enumerate(((0, P), (P, 3 * P))):
                        last = nc.vector.tensor_scalar(pr[:, lo:hi], pr[:, lo:hi], rinv[:, qt:qt + 1], None, ALU.mult)
                    last.then_inc(pr_ready, 1)

                def outputs(a):
                    n = 4 * g + a
                    dve.wait_ge(o_hi_ready, n + 1)
                    nc.vector.scalar_tensor_tensor(
                        out=oT_lo[:, bass.ds(n, 1), :].rearrange("p o t -> p (o t)"), in0=bank[4 + a % 2][:, 0:T],
                        scalar=small[:, bass.ds(gT_cols + KD + n, 1)],
                        in1=oT_hi[:, bass.ds(n, 1), :].rearrange("p o t -> p (o t)").bitcast(F32), op0=ALU.mult,
                        op1=ALU.subtract).then_inc(o_moved, 1)

                if part == 0 and s < 4:
                    scores(s)
                if part == 1 and s < 4:
                    probs(s)
                if part == 2 and 2 <= s < 6:
                    outputs(s - 2)

            def by_head(dst, first, n):
                dve.wait_ge(t_full, first + n + 1)
                nc.vector.tensor_copy(dst[:, n % 2 * 2:n % 2 * 2 + 2, :], tokens_of(bank[7][:, :])).then_inc(t_moved, 1)

            def period(h, s, attending):
                first = bank7_uses(h) + 4 if attending else 0
                if attending:
                    attend(h, s, 0)
                low(h, 2 * s + 4)
                if attending:
                    attend(h, s, 1)
                low(h, 2 * s + 5)
                if attending:
                    attend(h, s, 2)
                if s in (5, 6):
                    by_head(qT, first, s - 5)
                if s in (9, 10):
                    by_head(kT, first, s - 7)
                if s == 11:
                    for a in range(GROUP_H):
                        last = nc.vector.tensor_scalar(
                            gate_k[:, a, :], crow[:, :], pick_at(2 + GROUP_H * h + a),
                            pick_at(2 + HEADS + GROUP_H * h + a), ALU.mult, ALU.add)
                    last.then_inc(gate_k_ready, 1)

            def pick_at(col):
                return small[0:16, bass.ds(COLS["pick"].start + col, 1)]

            for s in range(SLOTS_QKV):
                if s == 2:
                    dve.wait_ge(squares, HALF)
                    rsqrt(1, ssq[:, 0:2], D)
                    nc.vector.tensor_scalar(rsq[:, :], rs[:, 0, :], SCALE, None, ALU.mult).then_inc(rs_ready, 1)
                period(0, s, False)
                if s == 4:
                    dve.wait_ge(small_pe, 2)
                    zb, neg, mag, ln1 = zf[:, 0, :], zf[:, 1, :], zf[:, 2, :], zf[:, 2, :]
                    for half in range(HALF):
                        cols = slice(half * FOX, (half + 1) * FOX)
                        own(nc.vector.scalar_tensor_tensor(
                            out=zb[:, cols], in0=bank[6][:, half * NARROW:half * NARROW + FOX],
                            scalar=rs[:, 0, half:half + 1], in1=of("bf")[:, cols], op0=ALU.mult, op1=ALU.add))
                    own(nc.vector.tensor_scalar(neg, zb, 0.0, None, ALU.min))
                    nc.vector.scalar_tensor_tensor(out=mag, in0=neg, scalar=-2.0, in1=zb, op0=ALU.mult,
                                                   op1=ALU.add).then_inc(small_dve, 1)
                if s == 6:
                    dve.wait_ge(small_act, 1)
                    halves = [v.rearrange("p (h n) -> p h n", h=HALF) for v in (neg, ln1)]
                    nc.vector.tensor_tensor(lf[:, :, 0:FOX], halves[0], halves[1], ALU.subtract)
                    nc.vector.tensor_tensor(lf[:, :, FOX:], halves[1], halves[0], ALU.subtract).then_inc(small_dve, 1)
                if s == 8:
                    dve.wait_ge(small_pe, 3)
                    own(nc.vector.tensor_copy(crow[:, :], bank[6][0:16, 0:T]))
                    nc.vector.tensor_scalar(gate_q[:, :], crow[:, :], pick[:, 0:1], pick[:, 1:2], ALU.mult,
                                            ALU.add).then_inc(small_dve, 1)
            with dve.Fori(1, HEAD_GROUPS) as h:
                for s in range(SLOTS_QKV):
                    period(h, s, True)

            def add_out(kind, cb):
                i = OUT_ORDER.index((kind, cb, 2 * kind + 1))
                dve.wait_ge(halves_used, 2 * (SLOTS_IN + i + 1))
                for h in range(HALF):
                    part = x[:, h, cb * 512:(cb + 1) * 512]
                    ins = nc.vector.scalar_tensor_tensor(
                        out=part, in0=bank[OUT_BANKS[kind, cb] + h][:, :], scalar=rs[:, 1 + kind, h:h + 1], in1=part,
                        op0=ALU.mult, op1=ALU.add)
                    ins.then_inc(x_added if kind else fox_added, 1)

            def new_xT(cb):
                for k in range(4 * cb, 4 * cb + 4):
                    dve.wait_ge(xt_hi, k - k % 2 + 2)
                    nc.vector.scalar_tensor_tensor(
                        out=hT_lo[:, k, :], in0=bank[XT_BANK[cb] + k % 4 // 2][:, k % 2 * T:(k % 2 + 1) * T],
                        scalar=gT[:, 2 * KD + k:2 * KD + k + 1], in1=hT_hi[:, k, :].bitcast(F32), op0=ALU.mult,
                        op1=ALU.subtract).then_inc(xt_moved, 1)

            for i in range(SLOTS_OUT):
                if i < 6:
                    attend(HEAD_GROUPS, i, 0)
                if 2 * i + 4 < 2 * SLOTS_OUT:
                    low(HEAD_GROUPS, 2 * i + 4)
                if i < 6:
                    attend(HEAD_GROUPS, i, 1)
                if 2 * i + 5 < 2 * SLOTS_OUT:
                    low(HEAD_GROUPS, 2 * i + 5)
                if i < 6:
                    attend(HEAD_GROUPS, i, 2)
                if i in (1, 8):
                    dve.wait_ge(sums_full, 1 + i // 8)
                    rsqrt(2 + i // 8, bank[5 if i == 1 else 7][:, 256:258], D // 2)
                    dve.sem_inc(sums_read, 1)
                if i in (2, 4, 6, 8):
                    add_out(0, i // 2 - 1)
                if i in (9, 11, 13, 15):
                    add_out(1, (i - 9) // 2)
                if i in (12, 14):
                    new_xT(i // 2 - 6)
            new_xT(2)
            dve.wait_ge(squares, HALF + 8)
            own(nc.vector.tensor_reduce(ssq[:, 10:12], ssq[:, 2:10].rearrange("p (h c) -> p h c", h=HALF),
                                        AX.X, ALU.add))
            rsqrt(4, ssq[:, 10:12], D)
            new_xT(3)

            TT, TR = nc.vector.tensor_tensor, nc.vector.tensor_reduce

            def over(v, n=4):
                return v.unsqueeze(2).to_broadcast([P, HALF, n])

            def first_best(hot, v, best, tmp, tmp1):
                own(TT(tmp, v, over(best), ALU.is_equal))
                own(TT(tmp, tmp, ramp.unsqueeze(1).to_broadcast([P, HALF, 4]), ALU.mult))
                own(TR(tmp1, tmp, AX.X, ALU.max))
                own(TT(hot, tmp, over(tmp1), ALU.is_equal))

            lg, le = rt[:, :, 40:44], rt[:, :, 44:60].rearrange("p h (g e) -> p h g e", g=NG)
            tmp, tmp1 = rt[:, :, 60:64], rt[:, :, 64]
            g_hot, e_sel, e_max, g_max = rt[:, :, 8:12], rt[:, :, 12:16], rt[:, :, 65], rt[:, :, 66]
            g_sum, p_group, e_sum = rt[:, :, 67], rt[:, :, 68], rt[:, :, 69]
            prob, rest, best = rt[:, :, 72:76], rt[:, :, 76:80], rt[:, :, 70]
            hot1, hot2, weight = rt[:, :, 80:84], rt[:, :, 84:88], rt[:, :, 88:92]
            wide4 = rt[:, :, 96:112].rearrange("p h (g e) -> p h g e", g=NG)

            dve.wait_ge(routed_pe, 1)
            for h in range(HALF):
                own(nc.vector.scalar_tensor_tensor(
                    out=rt[:, h, 40:60], in0=bank[4 + h][:, 0:NG + NE], scalar=rs[:, 3, h:h + 1],
                    in1=of("rb")[:, h * (NG + NE):(h + 1) * (NG + NE)], op0=ALU.mult, op1=ALU.add))
            own(TR(g_max, lg, AX.X, ALU.max))
            TT(rt[:, :, 0:4], lg, over(g_max), ALU.subtract).then_inc(small_dve, 1)
            first_best(g_hot, lg, g_max, tmp, tmp1)
            for h in range(HALF):
                own(TT(wide4[:, h], le[:, h], g_hot[:, h].unsqueeze(2).to_broadcast([P, NG, EG]), ALU.mult))
            for h in range(HALF):
                own(TR(e_sel[:, h], wide4[:, h].rearrange("p g e -> p e g"), AX.X, ALU.add))
            own(TR(e_max, e_sel, AX.X, ALU.max))
            TT(rt[:, :, 32:36], e_sel, over(e_max), ALU.subtract).then_inc(small_dve, 1)
            dve.wait_ge(small_act, 2)
            own(TR(g_sum, rt[:, :, 4:8], AX.X, ALU.add))
            own(nc.vector.reciprocal(p_group, g_sum))
            dve.wait_ge(small_act, 3)
            own(TR(e_sum, rt[:, :, 36:40], AX.X, ALU.add))
            own(nc.vector.reciprocal(e_sum, e_sum))
            own(TT(prob, rt[:, :, 36:40], over(e_sum), ALU.mult))
            own(TR(best, prob, AX.X, ALU.max))
            first_best(hot1, prob, best, tmp, tmp1)
            own(nc.vector.scalar_tensor_tensor(out=rest, in0=hot1, scalar=-2.0, in1=prob, op0=ALU.mult, op1=ALU.add))
            own(TR(best, rest, AX.X, ALU.max))
            first_best(hot2, rest, best, tmp, tmp1)
            own(TT(hot1, hot1, hot2, ALU.add))
            own(TT(weight, hot1, prob, ALU.mult))
            own(TR(tmp1, weight, AX.X, ALU.add))
            own(nc.vector.reciprocal(tmp1, tmp1))
            own(TT(weight, weight, over(tmp1), ALU.mult))
            own(TT(weight, weight, over(p_group), ALU.mult))
            for dst, chosen in ((mask, hot1), (comb, weight)):
                for h in range(HALF):
                    own(TT(dst[:, h, :].rearrange("p (g e) -> p g e", g=NG),
                           g_hot[:, h].unsqueeze(2).to_broadcast([P, NG, EG]),
                           chosen[:, h].unsqueeze(1).to_broadcast([P, NG, EG]), ALU.mult))
            nc.vector.tensor_copy(cmax[:, 0:1], ones[:, 0:1]).then_inc(small_dve, 1)
            dve.wait_ge(routed_pe, 2)
            ranks = bank[1][:, 0:HALF * NE].rearrange("p (h e) -> p h e", h=HALF)
            own(nc.vector.scalar_tensor_tensor(out=pos[:, :, :], in0=ranks, scalar=1.0, in1=mask[:, :, :],
                                               op0=ALU.add, op1=ALU.mult))
            own(nc.vector.tensor_scalar(pos[:, :, :], pos[:, :, :], -1.0, None, ALU.add))
            own(TR(cmax[:, 1:2], bank[1][:, 2 * NE:3 * NE], AX.X, ALU.max))
            own(nc.vector.tensor_scalar(cmax[:, 2:5], of("steps")[:, 0:3], cmax[:, 1:2], None, ALU.is_lt))
            own(TR(cmax[:, 5:6], cmax[:, 2:5], AX.X, ALU.add))
            nc.vector.tensor_scalar(n_pass[:, :], cmax[0:1, 5:6], 1.0, None, ALU.add).then_inc(pass_ready, 1)

            dve.wait_ge(pass_ready, 1)
            passes = dve.value_load(n_pass[0:1, 0:1], min_val=1, max_val=T // CAP)
            with dve.Fori(0, passes) as p:
                with dve.Fori(0, PAIRS) as i:
                    q = p * PAIRS + i
                    base = q * SLOTS_PAIR
                    dve.wait_ge(wt_full, FREE + q)
                    for dst in (pickD, pickW):
                        for half in range(HALF):
                            for e in range(2):
                                weight = rs[:, 3, half:half + 1] if dst is pickD else \
                                    comb[:, half, bass.ds(2 * i + e, 1)]
                                last = nc.vector.tensor_scalar(
                                    dst[:, half, e * CAP:(e + 1) * CAP], window, pos[:, half, bass.ds(2 * i + e, 1)],
                                    weight, ALU.is_equal, ALU.mult)
                        last.then_inc(picks, 1)
                    for c in range(4):
                        full, moved, n = ((b6_full, b6_moved, 7 * q), (b7_full, b7_moved, 6 * q))[c % 2]
                        dve.wait_ge(full, n + c // 2 + 1)
                        nc.vector.tensor_tensor(
                            xeT[:, 4 * c:4 * c + 4, :], bank[6 + c % 2][:, :].rearrange("p (k s) -> p k s", k=4),
                            gT[:, 2 * KD + 4 * c:2 * KD + 4 * c + 4].unsqueeze(2).to_broadcast([P, 4, P]),
                            ALU.mult).then_inc(moved, 1)
                    dve.wait_ge(wt_full, FREE + q + 1)
                    nc.vector.tensor_copy(pickWT[:, :], bank[2][:, 0:T]).then_inc(wt_moved, 1)
                    dve.wait_ge(gate_read, FREE + q + 1)
                    dve.wait_ge(moe_used, base + 16)
                    nc.vector.tensor_tensor(hid[:, :], sg[:, :], bank[1][:, :], ALU.mult).then_inc(hid_ready, 1)
                    dve.wait_ge(moe_used, base + SLOTS_PAIR)
                    for cb in range(2, 4):
                        nc.vector.tensor_copy(y_slots[:, cb * 512:(cb + 1) * 512],
                                              bank[2 + cb][:, :]).then_inc(y_moved_dve, 1)
                    dve.wait_ge(y_begun, HALF)
                    for n in range(8):
                        cb, h = divmod(n, HALF)
                        full, moved, at = ((b7_full, b7_moved, 6 * q + 2), (b6_full, b6_moved, 7 * q + 3))[n % 2]
                        dve.wait_ge(full, at + n // 2 + 1)
                        part = y_sum[:, h, cb * 512:(cb + 1) * 512]
                        nc.vector.tensor_tensor(part, part, bank[7 - n % 2][:, :], ALU.add).then_inc(moved, 1)
                nc.vector.tensor_scalar(window, window, float(CAP), None, ALU.add).then_inc(window_ready, 1)
                dve.wait_ge(window_ready, p + 1)

            dve.wait_ge(squares, HALF + 8 + HALF)
            rsqrt(5, ssq[:, 12:14], D)
            dve.wait_ge(gfin_loaded, 16)
            for h in range(HALF):
                nc.vector.scalar_tensor_tensor(out=x[:, h, :], in0=y_sum[:, h, :], scalar=rs[:, 4, h:h + 1],
                                               in1=gfin[:, :], op0=ALU.mult, op1=ALU.mult).then_inc(out_ready, 1)

        @block.tensor
        def _(pe):
            for s in (pv_full, wt_full):
                pe.sem_inc(s, FREE)

            def split_product(dst, lhs, rhs, k, cols, rhs_of, first, last):
                hi, lo = lhs[0][:, k, cols], lhs[1][:, k, cols]
                nc.tensor.matmul(dst, hi, rhs_of(rhs[0]), start=first, stop=False)
                nc.tensor.matmul(dst, hi, rhs_of(rhs[1]), start=False, stop=False)
                return nc.tensor.matmul(dst, lo, rhs_of(rhs[0]), start=False, stop=last)

            def half_product(h, n, lhs, dst, k0, k_first, k_last):
                pe.wait_ge(halves_split, 2 * SLOTS_QKV * h + n + 1)
                for half in range(HALF):
                    for kk in range(2):
                        last = split_product(bank[dst + half][:, :], lhs, (w_hi, w_lo), k0 + kk,
                                             slice(half * P, (half + 1) * P),
                                             lambda w, kk=kk: w[:, n % SPLITS, kk * 512:(kk + 1) * 512],
                                             k0 + kk == k_first, k0 + kk == k_last)
                last.then_inc(halves_used, 1)

            def narrow_product(dst, w, n, ks, first, last):
                for half in range(HALF):
                    for k in ks:
                        ins = split_product(dst[half], (hT_hi, hT_lo), w, k, slice(half * P, (half + 1) * P),
                                            lambda v, k=k: v[:, k * n:k * n + NARROW], k == first, k == last)
                return ins

            pe.wait_ge(small_loaded, 16)
            nc.tensor.matmul(bank[7][0:HEADS, 0:384], of("relT", BUCKETS + 1), of("onehot", BUCKETS + 1), start=True,
                             stop=True).then_inc(small_pe, 1)

            def attend(h, s):
                g = h - 1
                uses = bank7_uses(h)

                def scores(a):
                    if a == 0:
                        pe.wait_ge(t_moved, uses)
                        pe.wait_ge(gate_k_ready, h)
                    pe.wait_ge(s_moved, FREE + 4 * g + a)
                    for qt in range(HALF):
                        dst = bank[6][:, 0:P] if qt == 0 else bank[6][:, P:3 * P]
                        n = (qt + 1) * P
                        nc.tensor.matmul(dst, qT[:, a, qt * P:n], kT[:, a, 0:n], start=True, stop=False)
                        last = nc.tensor.matmul(dst, gate_q[:, qt * P:n], gate_k[:, a, 0:n], start=False, stop=True)
                    last.then_inc(s_full, 1)

                def values(a):
                    pe.wait_ge(t_moved, uses + a + 1)
                    pe.wait_ge(v_moved, 2 * h)
                    if a >= 2:
                        pe.wait_ge(o_moved, FREE + 4 * g + a - 1)
                    elif g == HEAD_GROUPS - 1 if isinstance(g, int) else False:
                        pe.wait_ge(sums_read, 1)
                    dst, v = bank[4 + a % 2], v_tok[:, :, a * HD:(a + 1) * HD]
                    nc.tensor.matmul(dst[:, 0:T], v[:, 0], prT[:, 0:T], start=True, stop=False)
                    nc.tensor.matmul(dst[:, P:T], v[:, 1], prT[:, T:T + P], start=False,
                                     stop=True).then_inc(pv_full, 1)

                def turn(a):
                    pe.wait_ge(pr_ready, FREE + 2 * (4 * g + a) + 2)
                    pe.wait_ge(t_moved, uses + a)
                    for n in range(3):
                        last = nc.tensor.transpose(bank[7][:, n * P:(n + 1) * P], pr[:, n * P:(n + 1) * P], ident)
                    last.then_inc(t_full, 1)

                if s < 4:
                    scores(s)
                if 2 <= s < 6:
                    values(s - 2)
                if 1 <= s < 5:
                    turn(s - 1)

            def by_head(h, first, moved, n):
                if n % 2 == 0:
                    pe.wait_ge(moved, 2 * h + 2)
                pe.wait_ge(t_moved, first + n)
                for a in range(2):
                    for half in range(HALF):
                        at = a * T + half * P
                        hd = (n % 2 * 2 + a) * HD
                        last = nc.tensor.transpose(bank[7][:, at:at + P], qk_tok[:, half, hd:hd + HD], ident)
                last.then_inc(t_full, 1)

            def period(h, s, attending):
                b, j = divmod(s, KD // KPS)
                first = bank7_uses(h) + 4 if attending else 0
                if attending and j == 0:
                    pe.wait_ge((q_moved, k_moved, v_moved)[b], 2 * h)
                    if b == 2:
                        pe.wait_ge(o_moved, FREE + 4 * h)
                if not attending and b == 0:
                    pe.wait_ge(hT_ready, 4 * (j + 1))
                for part in range(2):
                    half_product(h, 2 * s + part, (hT_hi, hT_lo), 2 * b, KPS * j + 2 * part, 0, KD - 1)
                if attending:
                    attend(h, s)
                if s in (5, 6):
                    by_head(h, first, q_moved, s - 5)
                if s in (9, 10):
                    by_head(h, first, k_moved, s - 7)

            for s in range(SLOTS_QKV):
                if s == 0:
                    pe.wait_ge(small_dve, 1)
                period(0, s, False)
                if s == 3:
                    pe.wait_ge(wsmall_ready, 1)
                    narrow_product([bank[6][:, half * NARROW:(half + 1) * NARROW] for half in range(HALF)],
                                   (wf_hi, wf_lo), FOX, range(KD), 0, KD - 1).then_inc(small_pe, 1)
                if s == 7:
                    pe.wait_ge(small_dve, 3)
                    nc.tensor.matmul(bank[6][0:16, 0:T], lf[:, 0, :], tri_ones, start=True, stop=False)
                    nc.tensor.matmul(bank[6][0:16, P:T], lf[:, 1, :], tri, start=False,
                                     stop=True).then_inc(small_pe, 1)
            pe.wait_ge(small_dve, 4)
            with pe.Fori(1, HEAD_GROUPS) as h:
                for s in range(SLOTS_QKV):
                    period(h, s, True)

            def sums(kind, dst):
                pe.wait_ge(sq_added, 1 + FOX * (kind + 1))
                for half in range(HALF):
                    last = nc.tensor.matmul(dst[:, T + half:T + half + 1], sqs[:, kind, half * P:(half + 1) * P],
                                            ones[:, 0:1], start=True, stop=True)
                last.then_inc(sums_full, 1)

            def new_xT(cb):
                pe.wait_ge(x_added, 2 * cb + 2)
                for k in range(4 * cb, 4 * cb + 4):
                    for half in range(HALF):
                        at = k % 2 * T + half * P
                        last = nc.tensor.transpose(bank[XT_BANK[cb] + k % 4 // 2][:, at:at + P],
                                                   x[:, half, k * P:(k + 1) * P], ident)
                    if k % 2:
                        last.then_inc(xt_full, 1)

            def route(cb):
                pe.wait_ge(xt_moved, 4 * cb + 4)
                return narrow_product([bank[4 + half][:, 0:NARROW] for half in range(HALF)], (wr_hi, wr_lo),
                                      NG + NE, range(4 * cb, 4 * cb + 4), 0, KD - 1)

            for i, (kind, cb, j) in enumerate(OUT_ORDER):
                dst = OUT_BANKS[kind, cb]
                if j == 2 * kind:
                    if i == 0:
                        for moved in (q_moved, k_moved, v_moved):
                            pe.wait_ge(moved, 2 * HEAD_GROUPS)
                    elif (kind, cb) in ((0, 2), (0, 3)):
                        pe.wait_ge(fox_added, 2 * cb - 2)
                    elif (kind, cb) in ((1, 2), (1, 3)):
                        pe.wait_ge(fox_added, 2 * cb + 2)
                    if (kind, cb) == (1, 0):
                        pe.wait_ge(o_moved, FREE + HEADS)
                    if (kind, cb) == (1, 1):
                        pe.wait_ge(sums_read, 2)
                for part in range(2):
                    half_product(HEAD_GROUPS, 2 * i + part, (oT_hi, oT_lo), dst, KPS * j + 2 * part, 8 * kind,
                                 8 * kind + 7)
                if i == 0:
                    sums(0, bank[5])
                if i == 7:
                    sums(1, bank[7])
                if i < 6:
                    attend(HEAD_GROUPS, i)
                if i in (11, 13):
                    new_xT((i - 11) // 2)
                if i in (12, 14):
                    route((i - 12) // 2)
                if i == 14:
                    new_xT(2)
            route(2)
            new_xT(3)
            route(3).then_inc(routed_pe, 1)

            pe.wait_ge(small_dve, 7)
            nc.tensor.matmul(bank[1][:, 0:NE], strict, mask[:, 0, :], start=True, stop=True)
            nc.tensor.matmul(bank[1][:, NE:2 * NE], ones, mask[:, 0, :], start=True, stop=False)
            nc.tensor.matmul(bank[1][:, NE:2 * NE], strict, mask[:, 1, :], start=False, stop=True)
            nc.tensor.matmul(bank[1][:, 2 * NE:3 * NE], ones, mask[:, 0, :], start=True, stop=False)
            nc.tensor.matmul(bank[1][:, 2 * NE:3 * NE], ones, mask[:, 1, :], start=False,
                             stop=True).then_inc(routed_pe, 1)

            pe.wait_ge(pass_ready, 1)
            passes = pe.value_load(n_pass[0:1, 0:1], min_val=1, max_val=T // CAP)
            with pe.Fori(0, passes) as p:
                with pe.Fori(0, PAIRS) as i:
                    q = p * PAIRS + i

                    def landed(j):
                        pe.wait_ge(moe_in[j % MOE_RING], 16 * (j // MOE_RING + 1) + q * (16 * SLOTS_PAIR // MOE_RING))
                        return moe_slot(j)

                    pe.wait_ge(picks, 2 * q + 1)
                    for c in range(4):
                        full, moved, n = ((b6_full, b6_moved, 7 * q), (b7_full, b7_moved, 6 * q))[c % 2]
                        pe.wait_ge(moved, FREE + n + c // 2)
                        for k in range(4):
                            for half in range(HALF):
                                kd = 4 * c + k
                                last = nc.tensor.matmul(bank[6 + c % 2][:, k * P:(k + 1) * P],
                                                        x[:, half, kd * P:(kd + 1) * P], pickD[:, half, :],
                                                        start=(half == 0), stop=(half == HALF - 1))
                        last.then_inc(full, 1)
                    pe.wait_ge(picks, 2 * q + 2)
                    pe.wait_ge(y_moved_act, FREE + 2 * q)
                    for half in range(HALF):
                        last = nc.tensor.transpose(bank[2][:, half * P:(half + 1) * P], pickW[:, half, :], ident)
                    last.then_inc(wt_full, 1)

                    pe.wait_ge(b6_moved, FREE + 7 * q + 2)
                    pe.wait_ge(b7_moved, FREE + 6 * q + 2)
                    pe.wait_ge(gate_read, FREE + q)
                    pe.wait_ge(hid_ready, FREE + q)
                    for m in range(2):
                        for j in range(KD // KPS):
                            at = 2 * (m * (KD // KPS) + j)
                            s = [landed(at + e) for e in range(2)]
                            for k in range(KPS):
                                kd = KPS * j + k
                                for e in range(2):
                                    last = nc.tensor.matmul(bank[m][e * CAP:(e + 1) * CAP, :],
                                                            xeT[:, kd, e * CAP:(e + 1) * CAP], s[e][:, k * 512:(k + 1) * 512],
                                                            start=(kd == 0), stop=(kd == KD - 1))
                                    if k == KPS - 1:
                                        last.then_inc(moe_used, 1)

                    pe.wait_ge(hid_ready, FREE + q + 1)
                    for k in range(KF):
                        last = nc.tensor.transpose(bank[6][:, k * P:(k + 1) * P], hid[:, k * P:(k + 1) * P], ident)
                    last.then_inc(b6_full, 1)
                    pe.wait_ge(b6_moved, FREE + 7 * q + 3)
                    pe.wait_ge(wt_moved, q + 1)
                    pe.wait_ge(y_moved_dve, FREE + 2 * q)
                    for k in range(KF):
                        s = [landed(2 * (2 * KD // KPS + k) + e) for e in range(2)]
                        for cb in range(4):
                            for e in range(2):
                                last = nc.tensor.matmul(bank[2 + cb][e * CAP:(e + 1) * CAP, :],
                                                        hidT[:, k, e * CAP:(e + 1) * CAP], s[e][:, cb * 512:(cb + 1) * 512],
                                                        start=(k == 0), stop=(k == KF - 1))
                                if cb == 3:
                                    last.then_inc(moe_used, 1)
                    for n in range(8):
                        cb, half = divmod(n, HALF)
                        full, moved, at = ((b7_full, b7_moved, 6 * q + 2), (b6_full, b6_moved, 7 * q + 3))[n % 2]
                        if half == 0:
                            pe.wait_ge(y_moved_act if cb < 2 else y_moved_dve, FREE + 2 * q + cb % 2 + 1)
                        pe.wait_ge(moved, FREE + at + n // 2)
                        nc.tensor.matmul(bank[7 - n % 2][:, :], pickWT[:, half * P:(half + 1) * P],
                                         y_slots[:, cb * 512:(cb + 1) * 512], start=True, stop=True).then_inc(full, 1)


def kernel(**inputs):
    import concourse.bacc as bacc
    from concourse.bass_utils import run_bass_kernel_spmd

    nc = bacc.Bacc("TRN2", target_bir_lowering=False, num_devices=1)
    i = {n: np.asarray(a) for n, a in inputs.items()}
    arrays = {
        "x": i["x"],
        "xT": i["x"][0].T.reshape(KD, P, T).transpose(1, 0, 2),
        "small": small_table(i),
        "w_in": i["w_in"], "w_out": i["w_out"], "w_gate": i["w_gate"], "w_up": i["w_up"], "w_down": i["w_down"],
        "g_final": i["final_norm_g"],
    }
    arrays = {f"in_{n}": np.ascontiguousarray(a) for n, a in arrays.items()}
    args = [nc.dram_tensor(n, a.shape, mybir.dt.from_np(a.dtype), kind="ExternalInput").ap()
            for n, a in arrays.items()]
    args.append(nc.dram_tensor("out", i["x"].shape, F32, kind="ExternalOutput").ap())
    layer(nc, *args)
    r = run_bass_kernel_spmd(nc, [arrays], core_ids=[0])
    return r.results[0]["out"]
```

```python
from contextlib import ExitStack

import numpy as np

import concourse.bass as bass
from concourse import mybir

ALU = mybir.AluOpType
ACT = mybir.ActivationFunctionType
AX = mybir.AxisListType
F32 = mybir.dt.float32
F32R = mybir.dt.float32r
I32 = mybir.dt.int32

P = 128
T = 256
HALF = T // P
D = 2048
KD = D // P
HD = 128
HEADS = 16
FOX = 8
GROUP_H = 4
HEAD_GROUPS = HEADS // GROUP_H
NE = 16
F = 512
KF = F // P
CAP = 64
PAIRS = NE // 2
NG = 4
EG = NE // NG
EPS = 1e-6
NEG = -1e30
BUCKETS = 32
SCALE = HD ** -0.5

SLOT = 2048
RING = 6
MOE_RING = 16
ONCE = 4
EARLY = 6
KPS = SLOT // 512
FREE = 1
SCATTERS = 8

SLOTS_QKV = 3 * KD // KPS
SLOTS_IN = HEAD_GROUPS * SLOTS_QKV
SLOTS_OUT = (D // 512) * KD // KPS
SLOTS_PAIR = 2 * (2 * KD // KPS + KF * D // SLOT)
SLOTS_PASS = PAIRS * SLOTS_PAIR
N_HALVES = 2 * (SLOTS_IN + SLOTS_OUT)
SPLITS = 4
HALF_SLOT = SLOT // 2
assert SLOTS_QKV % RING == 0 and 2 * SLOTS_PAIR % MOE_RING == 0

COLS, C_N = {}, 0
for _name, _n in (("gT", 3 * KD), ("relT", HEADS), ("onehot", 384), ("ident", P), ("tri", P), ("ones", P),
                  ("strict", P), ("window", CAP), ("ramp", 4), ("steps", 4), ("wf", KD * FOX + 24),
                  ("wr", KD * (NG + NE) + 12), ("bf", HALF * FOX), ("rb", HALF * (NG + NE)), ("add4", NG + NE)):
    COLS[_name] = slice(C_N, C_N + _n)
    C_N += _n
FIRST_COLS = COLS["onehot"].stop
QUAD = 32


def small_table(i):
    r = np.arange(P)
    table = np.zeros((P, C_N), np.float32)

    def put(name, a):
        a = np.asarray(a).reshape(len(a), -1)
        table[:a.shape[0], COLS[name].start:COLS[name].start + a.shape[1]] = a

    put("ident", np.eye(P))
    put("tri", r[:, None] <= r[None, :])
    put("ones", np.ones((P, P)))
    put("strict", r[:, None] < r[None, :])
    put("add4", r[:, None] % QUAD == np.arange(NG + NE)[None, :])
    put("window", np.tile(np.arange(CAP), (P, 1)))
    put("ramp", np.tile([4, 3, 2, 1], (P, 1)))
    put("steps", np.tile([CAP, 2 * CAP, 3 * CAP], (P, 1)))
    gains = np.concatenate([i[n].reshape(-1) for n in ("attn_norm_g", "fox_out_norm_g", "moba_out_norm_g",
                                                       "ffn_norm_g")])
    put("gT", gains.reshape(3 * KD, P).T)
    put("wf", i["w_in"][0, :, 3 * D:].reshape(KD, P, FOX).transpose(1, 0, 2))
    routers = np.concatenate([i["w_group_router"][0], i["w_expert_router"][0].reshape(D, NE)], 1)
    put("wr", routers.reshape(KD, P, NG + NE).transpose(1, 0, 2))
    put("bf", np.tile(i["b_forget"], (P, HALF)))
    put("rb", np.tile(np.concatenate([i["b_group_router"].reshape(-1), i["b_expert_router"].reshape(-1)]), (P, HALF)))
    relT = np.zeros((BUCKETS + 1, HEADS), np.float32)
    relT[:BUCKETS, FOX:] = i["rel_bias"].T
    relT[BUCKETS] = 1.0
    put("relT", relT)
    dist = np.arange(-(P - 1), T)
    d = np.maximum(dist, 0)
    exact = BUCKETS // 2
    ratio = np.log(np.maximum(d, 1).astype(np.float32) / exact) / np.log(128 / exact)
    large = np.minimum(exact + (ratio * (BUCKETS - exact)).astype(np.int32), BUCKETS - 1)
    bucket = np.where(d < exact, d, large)
    onehot = np.zeros((BUCKETS + 1, 384), np.float32)
    onehot[bucket[dist >= 0], np.nonzero(dist >= 0)[0]] = 1.0
    onehot[BUCKETS, :dist.size][dist < 0] = NEG
    put("onehot", onehot)
    return table


def layer(nc, x_in, xT_in, small_in, w_in, w_out, w_gate, w_up, w_down, g_final, out):
    ctx = ExitStack()
    with ctx:
        def sem(name):
            return ctx.enter_context(nc.semaphore(name))

        start, attention = ExitStack(), ExitStack()

        def sb(name, shape, dt=F32, until=ctx):
            return until.enter_context(nc.sbuf_tensor(name, shape, dt))

        sb("before_xT", [P, SPLITS * HALF_SLOT * 2 + KD * T], F32, start)
        xT = sb("xT", [P, KD, T], F32, start)
        start.close()
        w_hi = sb("w_hi", [P, SPLITS, HALF_SLOT], F32R, attention)
        w_lo = sb("w_lo", [P, SPLITS, HALF_SLOT], F32R, attention)
        oT_lo = sb("oT_lo", [P, KD, T], F32R, attention)
        oT_hi = sb("oT_hi", [P, KD, T], F32R, attention)
        hT_hi = sb("hT_hi", [P, KD, T], F32R, attention)
        hT_lo = sb("hT_lo", [P, KD, T], F32R, attention)
        attention.close()
        extra = sb("extra", [P, 4, SLOT])
        gfin = sb("gfin", [P, D])
        sg = sb("sg", [P, F])
        hid = sb("hid", [P, F])
        hidT = sb("hidT", [P, KF, P])
        pickD = sb("pickD", [P, HALF, 2 * CAP])
        pickW = sb("pickW", [P, HALF, 2 * CAP])
        y_sum = sb("y_sum", [P, HALF, D])
        early_a = sb("early_a", [P, 4, SLOT])

        attention = ExitStack()
        bias = sb("bias", [P, GROUP_H, 3 * P], F32, attention)
        windows = sb("windows", [P, GROUP_H, T], F32, attention)
        sc = sb("sc", [P, 384], F32, attention)
        pr = sb("pr", [P, 384], F32, attention)
        prT = sb("prT", [P, 384], F32, attention)
        crow = sb("crow", [HEADS, T], F32, attention)
        attention.close()
        early_b = sb("early_b", [P, 2, SLOT])

        ring = sb("ring", [P, RING, SLOT])
        x = sb("x", [P, HALF, D])
        both = sb("heads_rows", [P, 4096])
        newT = both[:, :].rearrange("p (k t) -> p k t", k=KD)
        heads = both[:, 0:2048]
        qT = heads[:, 0:1024].rearrange("p (a t) -> p a t", a=GROUP_H)
        kT = heads[:, 1024:2048].rearrange("p (a t) -> p a t", a=GROUP_H)
        xeT = heads[:, :].rearrange("p (k s) -> p k s", k=KD)
        rows = both[:, 2048:4096]
        c_keys = rows[:, 0:1024].rearrange("p (a t) -> p a t", a=GROUP_H)
        v_tok = rows[:, 1024:2048].rearrange("p (h n) -> p h n", h=HALF)
        y_slots = rows[:, :]
        small = sb("small", [P, C_N])

        def of(name, rows_=P):
            return small[0:rows_, COLS[name]]

        ident, tri, ones, strict = of("ident"), of("tri"), of("ones"), of("strict")
        tri_ones = small[:, COLS["tri"].start:COLS["ones"].stop]
        window, ramp, gT = of("window"), of("ramp"), of("gT")
        wf, wr = of("wf"), of("wr")
        band_dram = nc.dram_tensor("band_dram", [HEADS, 384], F32)
        c_dram = nc.dram_tensor("c_dram", [HEADS, T], F32)
        cneg = sb("cneg", [P, HALF, HEADS])
        rs_rows = sb("rs_rows", [P, T])
        rsq_rows = sb("rsq_rows", [P, T])
        pickWT = sb("pickWT", [P, T])
        lf = sb("lf", [P, HALF, 16])
        zf = sb("zf", [P, 4, 16])
        band = windows[0:HEADS, 0:2, :].rearrange("p a t -> p (a t)")[:, 0:384]
        nmx = sb("nmx", [P, 2])
        rsum = sb("rsum", [P, 2])
        rinv = sb("rinv", [P, 2])
        sq = sb("sq", [P, T])
        sqs = sb("sqs", [P, 2, T])
        ssq = sb("ssq", [P, 24])
        ms = sb("ms", [P, 2])
        sd = sb("sd", [P, 2])
        r0 = sb("r0", [P, 2])
        r1 = sb("r1", [P, 2])
        rs = sb("rs", [P, 5, 2])
        rt = sb("rt", [P, HALF, 160])
        mask = sb("mask", [P, HALF, NE])
        comb = sb("comb", [P, HALF, NE + 2])
        pos = sb("pos", [P, HALF, NE + 2])
        cmax = sb("cmax", [P, 8])
        less = sb("less", [P, HALF, NG + NE])
        n_pass = sb("n_pass", [1, 1], I32)

        bank = [ctx.enter_context(nc.psum_tensor(f"bank{i}", [P, 512], F32)) for i in range(8)]

        xT_in_s = [sem(f"xT_loaded{c}") for c in range(4)]
        x_loaded, gfin_loaded = sem("x_loaded"), sem("gfin_loaded")
        first_half_in = sem("first_half_in")
        parts_ready = sem("parts_ready")
        parts_moved = sem("parts_moved")
        first_loaded, small_loaded = sem("first_loaded"), sem("small_loaded")
        slot_in = [sem(f"slot_in{s}") for s in range(RING)]
        halves_hi, halves_split = sem("halves_hi"), sem("halves_split")
        halves_used = sem("halves_used")
        moe_in = [sem(f"moe_in{s}") for s in range(MOE_RING)]
        once_in = [sem(f"once_in{s}") for s in range(ONCE)]
        late_in = [sem(f"late_in{e}") for e in range(2)]
        down_full = sem("down_full")
        moe_used = sem("moe_used")
        hT_hi_ready, hT_ready = sem("hT_hi_ready"), sem("hT_ready")
        wsmall_ready = sem("wsmall_ready")
        band_stored, c_stored, bias_loaded = sem("band_stored"), sem("c_stored"), sem("bias_loaded")
        bias_ready = sem("bias_ready")
        squares = sem("squares")
        ms_ready, sd_ready = sem("ms_ready"), sem("sd_ready")
        small_pe, small_dve, small_act = sem("small_pe"), sem("small_dve"), sem("small_act")
        q_moved, k_moved, v_moved = sem("q_moved"), sem("k_moved"), sem("v_moved")
        t_full, t_moved = sem("t_full"), sem("t_moved")
        s_full, s_moved = sem("s_full"), sem("s_moved")
        nmx_ready, exps_ready, pr_ready = sem("nmx_ready"), sem("exps_ready"), sem("pr_ready")
        pv_full, o_hi_ready, o_moved = sem("pv_full"), sem("o_hi_ready"), sem("o_moved")
        sq_added = sem("sq_added")
        lf_zero = sem("lf_zero")
        sums_full = sem("sums_full")
        sums_read = sem("sums_read")
        fox_added = sem("fox_added")
        x_added = sem("x_added")
        xt_full = sem("xt_full")
        xt_moved_act, xt_moved_dve = sem("xt_moved_act"), sem("xt_moved_dve")
        routed_pe, pass_ready = sem("routed_pe"), sem("pass_ready")
        y_begun = sem("y_begun")
        pickD_ready, pickW_ready = sem("pickD_ready"), sem("pickW_ready")
        g_full, g_moved = sem("g_full"), sem("g_moved")
        hidT_full, hidT_moved = sem("hidT_full"), sem("hidT_moved")
        scat_full, scat_moved = sem("scat_full"), sem("scat_moved")
        wt_full, wt_moved = sem("wt_full"), sem("wt_moved")
        gate_read, hid_ready = sem("gate_read"), sem("hid_ready")
        y_moved_act, y_moved_dve = sem("y_moved_act"), sem("y_moved_dve")
        out_ready, out_stored = sem("out_ready"), sem("out_stored")
        window_ready = sem("window_ready")
        dve_step, act_step = sem("dve_step"), sem("act_step")

        block = ctx.enter_context(nc.Block())

        w_in_v = w_in.rearrange("o (j k p) n -> (o p) j k n", p=P, k=KPS)
        w_out_v = w_out.rearrange("o (j k p) n -> (o p) j k n", p=P, k=KPS)
        w_gate_v = w_gate.rearrange("o e (j k p) f -> p (o e) j k f", p=P, k=KPS)
        w_up_v = w_up.rearrange("o e (j k p) f -> p (o e) j k f", p=P, k=KPS)
        w_down_v = w_down.rearrange("o e (k p) d -> p (o e) k d", p=P)
        gT_cols = COLS["gT"].start

        OUT_ORDER = [(kind, cb, 2 * kind + j) for kind in range(2) for cb in range(4) for j in range(2)]
        GATHER_BANKS = (6, 7, 4, 5)
        LAST_BANKS = (0, 1, 6, 7)
        XT_BANK = {0: 4, 1: 6, 2: 6, 3: 0}
        OUT_BANKS = {(0, 0): 0, (0, 1): 2, (0, 2): 0, (0, 3): 2, (1, 0): 4, (1, 1): 6, (1, 2): 0, (1, 3): 2}

        OVER_FOX = (MOE_RING, MOE_RING + 2)

        def moe_slot(j, first=False):
            if first and MOE_RING <= j < MOE_RING + ONCE:
                s = j - MOE_RING
                return (y_sum[:, 0, :], y_sum[:, 1, :], gfin[:, :], y_slots)[s], once_in[s], 0
            turn, s = divmod(j if first and j < MOE_RING else j - ONCE, MOE_RING)
            if s < EARLY:
                to = early_a[:, s, :] if s < 4 else early_b[:, s - 4, :]
            elif s < EARLY + RING:
                to = ring[:, (SLOTS_IN + SLOTS_OUT + s - EARLY) % RING, :]
            else:
                to = extra[:, (0, 2, 1, 3)[s - EARLY - RING], :]
            return to, moe_in[s], turn

        def tokens_of(cols):
            return cols.rearrange("p (k t) -> p k t", k=2)

        class Own:

            def __init__(self, eng, own):
                self.eng, self.own, self.n = eng, own, 0

            def __call__(self, ins):
                self.n += 1
                ins.then_inc(self.own, 1)
                self.eng.wait_ge(self.own, self.n)

        def half_block(n):
            s, part = divmod(n, 2)
            return s, s % RING, slice(part * HALF_SLOT, (part + 1) * HALF_SLOT)

        @block.sync
        def _(sp):
            def qkv_load(hg, s, first):
                b, j = divmod(s, KD // KPS)
                kind, half = divmod(hg, 2) if first else (hg // 2, hg % 2)
                col = kind * 3072 + half * 512 + b * 1024
                if not first or s >= RING:
                    sp.wait_ge(halves_split, 2 * (hg * SLOTS_QKV + s - RING + 1))
                sp.dma_start(ring[:, s % RING, :].rearrange("p (k n) -> p k n", k=KPS),
                             w_in_v[:, j, :, bass.ds(col, 512)]).then_inc(slot_in[s % RING], 16)

            sp.dma_start(small[:, 0:FIRST_COLS], small_in[:, 0:FIRST_COLS]).then_inc(first_loaded, 16)
            def xT_load(c):
                sp.dma_start(xT[:, 4 * c:4 * c + 4, :], xT_in[:, 4 * c:4 * c + 4, :]).then_inc(xT_in_s[c], 16)

            xT_load(0)
            for part, landed in enumerate((first_half_in, slot_in[0])):
                sp.dma_start(ring[:, 0, part * HALF_SLOT:(part + 1) * HALF_SLOT].rearrange("p (k n) -> p k n", k=2),
                             w_in_v[:, 0, 2 * part:2 * part + 2, 0:512]).then_inc(landed, 16)
            xT_load(1)
            qkv_load(0, 1, True)
            xT_load(2)
            xT_load(3)
            qkv_load(0, 2, True)
            sp.dma_start(small[:, FIRST_COLS:], small_in[:, FIRST_COLS:]).then_inc(small_loaded, 16)
            for s in range(3, SLOTS_QKV):
                qkv_load(0, s, True)
                if s == 4:
                    for h in range(HALF):
                        sp.dma_start(x[:, h, :], x_in[0, h * P:(h + 1) * P, :]).then_inc(x_loaded, 16)
            with sp.Fori(1, HEAD_GROUPS) as hg:
                for s in range(SLOTS_QKV):
                    qkv_load(hg, s, False)

            def moe_operands(j, pair, j_in_pair, first):
                c, e = divmod(j_in_pair, 2)
                n = KD // KPS
                w, c = ((w_gate_v, c), (w_up_v, c - n), (w_down_v, c - 2 * n))[min(c // n, 2)]
                src = w[:, bass.ds(2 * pair + e, 1), c]
                dst, landed, _ = moe_slot(j, first)
                if w is w_down_v:
                    return dst, src.rearrange("p o d -> p (o d)"), landed
                return dst.rearrange("p (k f) -> p k f", k=KPS), src.rearrange("p o k f -> p (o k) f"), landed

            def moe_load(j, pair, j_in_pair, first=False):
                if j_in_pair < SLOTS_PAIR - 1:
                    dst, src, landed = moe_operands(j, pair, j_in_pair, first)
                    sp.dma_start(dst, src).then_inc(landed, 16)
                else:
                    two = [moe_operands(j - 1 + e, pair, j_in_pair - 1 + e, first) for e in range(2)]
                    for part in range(2):
                        cols = slice(part * HALF_SLOT, (part + 1) * HALF_SLOT)
                        for (dst, src, landed), late in zip(two, late_in):
                            sp.dma_start(dst[:, cols], src[:, cols]).then_inc(late if part else landed, 16)

            for i, (_, cb, j) in enumerate(OUT_ORDER):
                n = SLOTS_IN + i
                sp.wait_ge(halves_split, 2 * (n - RING + 1))
                sp.dma_start(ring[:, n % RING, :].rearrange("p (k n) -> p k n", k=KPS),
                             w_out_v[:, j, :, cb * 512:(cb + 1) * 512]).then_inc(slot_in[n % RING], 16)
                if i == 7:
                    sp.wait_ge(halves_used, 2 * SLOTS_IN)
                if i == SLOTS_OUT - 1:
                    sp.wait_ge(halves_used, 2 * (SLOTS_IN + SLOTS_OUT // 2))
                    for j in OVER_FOX:
                        moe_load(j, 0, j, True)
                if i in (7, 9):
                    moe_load(i - 7, 0, i - 7, True)
                    moe_load(i - 6, 0, i - 6, True)
                if i == 12:
                    sp.wait_ge(pv_full, FREE + HEADS)
                    moe_load(4, 0, 4, True)
                    moe_load(5, 0, 5, True)

            def body_loads(body, base, first=False):
                for j in range(EARLY if first else 0, 2 * SLOTS_PAIR):
                    if j % SLOTS_PAIR == SLOTS_PAIR - 2 or first and j in OVER_FOX:
                        continue
                    if first and j < EARLY + RING:
                        sp.wait_ge(halves_split, 2 * (SLOTS_IN + SLOTS_OUT - RING + 1 + j - EARLY))
                    elif first and j < EARLY + RING + 2:
                        sp.wait_ge(halves_used, N_HALVES - 2)
                    elif first and j < MOE_RING + ONCE:
                        sp.wait_ge(halves_used, N_HALVES)
                        if j == MOE_RING + ONCE - 1:
                            sp.wait_ge(parts_ready, 1)
                    elif first and j < 2 * MOE_RING + ONCE:
                        sp.wait_ge(moe_used, j - ONCE - MOE_RING + 1)
                    else:
                        sp.wait_ge(moe_used, base + (j - MOE_RING + 1))
                    moe_load(j, 2 * body + j // SLOTS_PAIR, j % SLOTS_PAIR, first)

            body_loads(0, 0, True)
            with sp.Fori(1, PAIRS // 2) as body:
                body_loads(body, body * (2 * SLOTS_PAIR))
            sp.wait_ge(pass_ready, 1)
            passes = sp.value_load(n_pass[0:1, 0:1], min_val=1, max_val=T // CAP)
            with sp.If(passes > 1):
                with sp.Fori(1, passes) as p:
                    with sp.Fori(0, PAIRS // 2) as body:
                        body_loads(body, p * SLOTS_PASS + body * (2 * SLOTS_PAIR))
            for n in range(4):
                h, cols = n // 2, slice(n % 2 * (D // 2), (n % 2 + 1) * (D // 2))
                sp.wait_ge(out_ready, n + 1)
                sp.dma_start(out[0, h * P:(h + 1) * P, cols], x[:, h, cols]).then_inc(out_stored, 16)
            sp.wait_ge(out_stored, 16 * 4)

        @block.scalar
        def _(act):
            own = Own(act, act_step)
            for s in (exps_ready, gate_read, y_moved_act, t_moved):
                act.sem_inc(s, FREE)

            def root(k, cols=slice(0, 2)):
                act.wait_ge(ms_ready, k)
                nc.scalar.activation(sd[:, cols], ms[:, cols], ACT.Sqrt).then_inc(sd_ready, 1)

            def high(h, n):
                s, at, cols = half_block(n)
                done = 2 * SLOTS_QKV * h + n
                if isinstance(h, int) and done == 0:
                    act.wait_ge(first_half_in, 16)
                else:
                    act.wait_ge(slot_in[at], 16 * (SLOTS_QKV // RING * h + s // RING + 1))
                if not (isinstance(h, int) and done < SPLITS):
                    act.wait_ge(halves_used, done - SPLITS + 1)
                nc.scalar.activation(w_hi[:, n % SPLITS, :], ring[:, at, cols], ACT.Copy).then_inc(halves_hi, 1)

            act.wait_ge(lf_zero, 1)
            nc.scalar.activation(sd[:, :], lf[:, 0, FOX:FOX + 2], ACT.Copy)
            act.wait_ge(first_loaded, 16)
            for k in range(KD):
                if k % 4 == 0:
                    act.wait_ge(xT_in_s[k // 4], 16)
                nc.scalar.activation(hT_hi[:, k, :], xT[:, k, :], ACT.Copy,
                                     scale=gT[:, k:k + 1]).then_inc(hT_hi_ready, 1)
                if k in (1, 3, 6, 7):
                    high(0, (1, 3, 6, 7).index(k))

            def attend(h, s):
                g = h - 1

                def turned(a):
                    act.wait_ge(t_full, FREE + 4 * g + a + 1)
                    act.wait_ge(pv_full, FREE + 4 * g + a)
                    nc.scalar.activation(prT[:, :], bank[7][:, 0:3 * P], ACT.Copy).then_inc(t_moved, 1)

                def exps(a):
                    act.wait_ge(nmx_ready, 4 * g + a + 1)
                    act.wait_ge(t_full, FREE + 4 * g + a)
                    for qt, (lo, hi) in enumerate(((0, P), (P, 3 * P))):
                        last = nc.scalar.activation(pr[:, lo:hi], sc[:, lo:hi], ACT.Exp, bias=nmx[:, qt:qt + 1],
                                                    accum_out=rsum[:, qt:qt + 1])
                    last.then_inc(exps_ready, 1)

                def outputs(a):
                    n = 4 * g + a
                    act.wait_ge(pv_full, FREE + n + 1)
                    act.wait_ge(sq_added, 1 + n)
                    src = bank[4 + a % 2][:, 0:T]
                    nc.scalar.activation(oT_hi[:, bass.ds(n, 1), :].rearrange("p o t -> p (o t)"), src, ACT.Copy,
                                         scale=small[:, bass.ds(gT_cols + KD + n, 1)])
                    nc.scalar.activation(sq[:, :], src, ACT.Square).then_inc(o_hi_ready, 1)

                if 1 <= s <= 4:
                    turned(s - 1)
                if s < 4:
                    exps(s)
                if 2 <= s < 6:
                    outputs(s - 2)

            def period(h, s, attending):
                high(h, 2 * s + 4)
                if attending:
                    attend(h, s)
                high(h, 2 * s + 5)
                if s == SLOTS_QKV - 1:
                    act.wait_ge(halves_used, 2 * SLOTS_QKV * h + 2 * s + 2)
                    if attending:
                        act.wait_ge(pv_full, FREE + 4 * h)
                    for half in range(HALF):
                        nc.scalar.activation(v_tok[:, half, :], bank[4 + half][:, :], ACT.Copy,
                                             scale=rs[:, 0, half:half + 1]).then_inc(v_moved, 1)

            for s in range(SLOTS_QKV):
                if s == 4:
                    act.wait_ge(x_loaded, 16 * HALF)
                    for h in range(HALF):
                        nc.scalar.activation((heads, rows)[h][:, :], x[:, h, :], ACT.Square,
                                             accum_out=ssq[:, h:h + 1]).then_inc(squares, 1)
                    root(1)
                if s == SLOTS_QKV - 1:
                    act.wait_ge(small_dve, 3)
                period(0, s, False)
                if s == 6:
                    act.wait_ge(small_dve, 4)
                    own(nc.scalar.activation(zf[:, 3, :], zf[:, 2, :], ACT.Exp, scale=-1.0))
                    nc.scalar.activation(zf[:, 2, :], zf[:, 3, :], ACT.Ln, bias=1.0).then_inc(small_act, 1)
            with act.Fori(1, HEAD_GROUPS) as h:
                for s in range(SLOTS_QKV):
                    period(h, s, True)

            def new_x(cb):
                for h in range(HALF):
                    act.wait_ge(x_added, 2 * cb + h + 1)
                    act.wait_ge(squares, HALF + 2 * cb + h)
                    part = slice(cb * 512, (cb + 1) * 512)
                    nc.scalar.activation(sqs[:, :, :].rearrange("p o t -> p (o t)"), x[:, h, part], ACT.Square,
                                         accum_out=ssq[:, 2 + 4 * h + cb:3 + 4 * h + cb]).then_inc(squares, 1)

            def new_xT(cb):
                act.wait_ge(xt_full, 2 * cb + 1)
                nc.scalar.activation(newT[:, 4 * cb:4 * cb + 2, :], tokens_of(bank[XT_BANK[cb]][:, :]),
                                     ACT.Copy).then_inc(xt_moved_act, 1)

            for i in range(SLOTS_OUT):
                if i in (12, 14):
                    new_xT(i // 2 - 6)
                if 2 * i + 4 < 2 * SLOTS_OUT:
                    high(HEAD_GROUPS, 2 * i + 4)
                if i < 6:
                    attend(HEAD_GROUPS, i)
                if 2 * i + 5 < 2 * SLOTS_OUT:
                    high(HEAD_GROUPS, 2 * i + 5)
                if i == 1:
                    root(2)
                if i == 8:
                    root(3)
                if i in (11, 13, 15):
                    new_x(i // 2 - 5)
            new_xT(2)
            new_x(3)
            new_xT(3)
            root(4)
            act.wait_ge(small_dve, 8)
            nc.scalar.activation(less[:, :, :], less[:, :, :], ACT.Exp).then_inc(small_act, 1)


            def pair(q, first=False):
                base = q * SLOTS_PAIR
                act.wait_ge(moe_used, base + 8)
                act.wait_ge(hid_ready, FREE + q)
                nc.scalar.activation(sg[:, :], bank[0][:, :], ACT.Silu).then_inc(gate_read, 1)
                act.wait_ge(hidT_full, q + 1)
                nc.scalar.activation(hidT[:, :, :].rearrange("p k s -> p (k s)"), bank[6][:, :],
                                     ACT.Copy).then_inc(hidT_moved, 1)
                for cb in range(2):
                    act.wait_ge(down_full, 3 * q + cb + 1)
                    nc.scalar.activation(y_slots[:, cb * 512:(cb + 1) * 512], bank[2 + cb][:, :],
                                         ACT.Copy).then_inc(y_moved_act, 1)
                if first:
                    act.wait_ge(moe_used, SLOTS_PAIR)
                    act.dma_start(gfin[:, :], g_final.partition_broadcast(P)).then_inc(gfin_loaded, 16)
                    for h in range(HALF):
                        nc.scalar.activation(y_sum[:, h, :], x[:, h, :], ACT.Copy).then_inc(y_begun, 1)

            pair(0, True)
            act.wait_ge(pass_ready, 1)
            passes = act.value_load(n_pass[0:1, 0:1], min_val=1, max_val=T // CAP)
            with act.Fori(1, passes * PAIRS) as q:
                pair(q)

            nc.scalar.activation(sd[:, :], ms[:, :], ACT.Sqrt).then_inc(sd_ready, 1)
            for n in range(8):
                h, cb = divmod(n, 4)
                act.wait_ge(scat_moved, passes * (SCATTERS * PAIRS) + n + 1)
                if n >= 2:
                    act.wait_ge(squares, HALF + 8 + n - 1)
                nc.scalar.activation((sg, hid)[n % 2][:, :], y_sum[:, h, cb * 512:(cb + 1) * 512], ACT.Square,
                                     accum_out=ssq[:, 12 + n:13 + n]).then_inc(squares, 1)
                if n == 5:
                    root(5, slice(0, 1))
            root(6, slice(1, 2))

        @block.gpsimd
        def _(pool):
            nc.gpsimd.memset(lf[:, :, FOX:], 0.0).then_inc(lf_zero, 1)
            nc.gpsimd.memset(sqs[:, :, :], 0.0).then_inc(sq_added, 1)
            pool.wait_ge(first_loaded, 16)
            pool.wait_ge(small_loaded, 16)
            for w, n, gains in ((wf, FOX, gT[:, 0:KD]), (wr, NG + NE, gT[:, 2 * KD:3 * KD])):
                by_block = w[:, 0:KD * n].rearrange("p (k n) -> p k n", k=KD)
                nc.gpsimd.tensor_tensor(by_block, by_block, gains.unsqueeze(2).to_broadcast([P, KD, n]),
                                        ALU.mult).then_inc(wsmall_ready, 1)
            pool.wait_ge(small_dve, 1)
            pool.dma_start(band_dram.ap(), band).then_inc(band_stored, 16)
            pool.wait_ge(band_stored, 16)
            band_v = bass.AP(tensor=band_dram, offset=0, ap=[[1, P], [384, HEADS], [1, T]])
            c_v = bass.AP(tensor=c_dram, offset=0, ap=[[0, P], [T, HEADS], [1, T]])
            pool.dma_start(windows[:, :, :], band_v[:, 0:GROUP_H, :]).then_inc(bias_loaded, 16)
            pool.wait_ge(small_dve, 6)
            pool.dma_start(c_dram.ap(), crow[:, :]).then_inc(c_stored, 16)
            pool.wait_ge(c_stored, 16)
            pool.dma_start(c_keys[:, :, :], c_v[:, 0:GROUP_H, :]).then_inc(bias_loaded, 16)

            def group_bias(g):
                pool.wait_ge(bias_loaded, 32 * (g + 1))
                if g:
                    pool.wait_ge(s_moved, FREE + 4 * g)
                for lo, hi in ((0, P), (P, 3 * P)):
                    last = nc.gpsimd.tensor_tensor(bias[:, :, lo:hi], windows[:, :, 0:hi - lo][:, :, ::-1],
                                                   c_keys[:, :, 0:hi - lo], ALU.add)
                last.then_inc(bias_ready, 1)
                if g < HEAD_GROUPS - 1:
                    pool.wait_ge(bias_ready, g + 1)
                    cols = slice(GROUP_H * (g + 1), GROUP_H * (g + 2))
                    pool.dma_start(windows[:, :, :], band_v[:, cols, :]).then_inc(bias_loaded, 16)
                    pool.dma_start(c_keys[:, :, :], c_v[:, cols, :]).then_inc(bias_loaded, 16)

            group_bias(0)
            for n in range(HEADS):
                pool.wait_ge(o_hi_ready, n + 1)
                pool.wait_ge(sq_added, 1 + n)
                dst = sqs[:, n // FOX, :]
                nc.gpsimd.tensor_tensor(dst, dst, sq[:, :], ALU.add).then_inc(sq_added, 1)
                if n % GROUP_H == GROUP_H - 1 and n < HEADS - 1:
                    group_bias(n // GROUP_H + 1)

        @block.vector
        def _(dve):
            own = Own(dve, dve_step)
            for s in (s_moved, y_moved_dve, hid_ready, pr_ready, o_moved):
                dve.sem_inc(s, FREE)
            dve.sem_inc(scat_moved, SCATTERS)

            def rsqrt(k, sums, width, row=None, cols=slice(0, 2), beside=None):
                nc.vector.tensor_scalar(ms[:, cols], sums, 1.0 / width, EPS, ALU.mult, ALU.add).then_inc(ms_ready, 1)
                if beside:
                    beside()
                dve.wait_ge(ms_ready, k)
                dve.wait_ge(sd_ready, k + (k > 4))
                guess, error = r0[:, cols], r1[:, cols]
                own(nc.vector.reciprocal(guess, sd[:, cols]))
                own(nc.vector.tensor_tensor(error, guess, guess, ALU.mult))
                own(nc.vector.tensor_tensor(error, error, ms[:, cols], ALU.mult))
                own(nc.vector.tensor_scalar(error, error, -0.5, 1.5, ALU.mult, ALU.add))
                own(nc.vector.tensor_tensor(rs[:, k - 1 if row is None else row, cols], guess, error, ALU.mult))

            def low(h, n):
                s, at, cols = half_block(n)
                done = 2 * SLOTS_QKV * h + n
                dve.wait_ge(halves_hi, done + 1)
                ins = nc.vector.tensor_tensor(w_lo[:, n % SPLITS, :], ring[:, at, cols],
                                              w_hi[:, n % SPLITS, :].bitcast(F32), ALU.subtract)
                ins.then_inc(halves_split, 1)

            dve.wait_ge(small_pe, 1)
            nc.vector.tensor_copy(band, bank[7][0:HEADS, 0:384]).then_inc(small_dve, 1)
            for k in range(KD):
                dve.wait_ge(hT_hi_ready, k + 1)
                nc.vector.scalar_tensor_tensor(out=hT_lo[:, k, :], in0=xT[:, k, :], scalar=gT[:, k:k + 1],
                                               in1=hT_hi[:, k, :].bitcast(F32), op0=ALU.mult,
                                               op1=ALU.subtract).then_inc(hT_ready, 1)
                if k in (1, 3, 6, 7):
                    low(0, (1, 3, 6, 7).index(k))

            def attend(h, s, part):
                g = h - 1

                def scores(a):
                    dve.wait_ge(s_full, 4 * g + a + 1)
                    if a == 0:
                        dve.wait_ge(bias_ready, g + 1)
                    dve.wait_ge(exps_ready, FREE + 4 * g + a)
                    for qt, (lo, hi) in enumerate(((0, P), (P, 3 * P))):
                        last = nc.vector.scalar_tensor_tensor(
                            out=sc[:, lo:hi], in0=bank[6][:, lo:hi], scalar=cneg[:, qt, bass.ds(4 * g + a, 1)],
                            in1=bias[:, a, lo:hi], op0=ALU.subtract, op1=ALU.add)
                    last.then_inc(s_moved, 1)
                    dve.wait_ge(s_moved, FREE + 4 * g + a + 1)
                    for qt, (lo, hi) in enumerate(((0, P), (P, 3 * P))):
                        last = nc.vector.tensor_reduce(nmx[:, qt:qt + 1], sc[:, lo:hi], AX.X, ALU.max, negate=True)
                    last.then_inc(nmx_ready, 1)

                def probs(a):
                    dve.wait_ge(exps_ready, FREE + 4 * g + a + 1)
                    nc.vector.reciprocal(rinv[:, :], rsum[:, :]).then_inc(pr_ready, 1)
                    dve.wait_ge(pr_ready, FREE + 2 * (4 * g + a) + 1)
                    for qt, (lo, hi) in enumerate(((0, P), (P, 3 * P))):
                        last = nc.vector.tensor_scalar(pr[:, lo:hi], pr[:, lo:hi], rinv[:, qt:qt + 1], None, ALU.mult)
                    last.then_inc(pr_ready, 1)

                def outputs(a):
                    n = 4 * g + a
                    dve.wait_ge(o_hi_ready, n + 1)
                    nc.vector.scalar_tensor_tensor(
                        out=oT_lo[:, bass.ds(n, 1), :].rearrange("p o t -> p (o t)"), in0=bank[4 + a % 2][:, 0:T],
                        scalar=small[:, bass.ds(gT_cols + KD + n, 1)],
                        in1=oT_hi[:, bass.ds(n, 1), :].rearrange("p o t -> p (o t)").bitcast(F32), op0=ALU.mult,
                        op1=ALU.subtract).then_inc(o_moved, 1)

                if part == 0 and s < 4:
                    scores(s)
                if part == 1 and s < 4:
                    probs(s)
                if part == 2 and 2 <= s < 6:
                    outputs(s - 2)

            def by_head(h, s, dst, first_bank, scale, moved):
                dve.wait_ge(halves_used, 2 * SLOTS_QKV * h + 2 * s)
                for n in range(2):
                    nc.vector.tensor_tensor(dst[:, 2 * n:2 * n + 2, :], tokens_of(bank[first_bank + n][:, :]),
                                            scale[:, :].unsqueeze(1).to_broadcast([P, 2, T]),
                                            ALU.mult).then_inc(moved, 1)

            def period(h, s, attending):
                if attending:
                    attend(h, s, 0)
                low(h, 2 * s + 4)
                if attending:
                    attend(h, s, 1)
                low(h, 2 * s + 5)
                if attending:
                    attend(h, s, 2)
                if s == 7:
                    if attending:
                        dve.wait_ge(s_full, 4 * h)
                    by_head(h, 4, qT, 0, rsq_rows, q_moved)
                if s == 9:
                    by_head(h, 8, kT, 2, rs_rows, k_moved)

            for s in range(SLOTS_QKV):
                if s == 4:
                    dve.wait_ge(small_pe, 2)
                    nc.vector.tensor_copy(sc[:, 0:T], bank[6][:, 0:T]).then_inc(small_dve, 1)
                    dve.wait_ge(squares, HALF)
                    rsqrt(1, ssq[:, 0:2], D)
                    for half in range(HALF):
                        last = nc.vector.tensor_scalar(pr[:, half * P:(half + 1) * P], ident,
                                                       rs[:, 0, half:half + 1], None, ALU.mult)
                    last.then_inc(small_dve, 1)
                if s == 6:
                    dve.wait_ge(small_pe, 4)
                    nc.vector.tensor_copy(rs_rows[:, :], bank[7][:, 0:T])
                    own(nc.vector.tensor_scalar(rsq_rows[:, :], bank[7][:, 0:T], SCALE, None, ALU.mult))
                period(0, s, False)
                if s == 5:
                    dve.wait_ge(small_pe, 3)
                    zb, neg, mag, ln1 = zf[:, 0, :], zf[:, 1, :], zf[:, 2, :], zf[:, 2, :]
                    for half in range(HALF):
                        cols = slice(half * FOX, (half + 1) * FOX)
                        own(nc.vector.scalar_tensor_tensor(
                            out=zb[:, cols], in0=bank[6][:, T + half * QUAD:T + half * QUAD + FOX],
                            scalar=rs[:, 0, half:half + 1], in1=of("bf")[:, cols], op0=ALU.mult, op1=ALU.add))
                    own(nc.vector.tensor_scalar(neg, zb, 0.0, None, ALU.min))
                    nc.vector.scalar_tensor_tensor(out=mag, in0=neg, scalar=-2.0, in1=zb, op0=ALU.mult,
                                                   op1=ALU.add).then_inc(small_dve, 1)
                if s == 7:
                    dve.wait_ge(small_act, 1)
                    dve.wait_ge(lf_zero, 1)
                    by_half = [v.rearrange("p (h n) -> p h n", h=HALF) for v in (neg, ln1)]
                    nc.vector.tensor_tensor(lf[:, :, 0:FOX], by_half[1], by_half[0], ALU.subtract).then_inc(small_dve, 1)
                if s == 9:
                    dve.wait_ge(small_pe, 5)
                    nc.vector.tensor_copy(crow[:, :], bank[6][0:HEADS, 0:T])
                    nc.vector.tensor_copy(cneg[:, :, :], bank[6][:, T:T + HALF * HEADS].rearrange(
                        "p (h n) -> p h n", h=HALF)).then_inc(small_dve, 1)
            with dve.Fori(1, HEAD_GROUPS) as h:
                for s in range(SLOTS_QKV):
                    period(h, s, True)

            def add_out(kind, cb):
                i = OUT_ORDER.index((kind, cb, 2 * kind + 1))
                dve.wait_ge(halves_used, 2 * (SLOTS_IN + i + 1))
                for h in range(HALF):
                    part = x[:, h, cb * 512:(cb + 1) * 512]
                    ins = nc.vector.scalar_tensor_tensor(
                        out=part, in0=bank[OUT_BANKS[kind, cb] + h][:, :], scalar=rs[:, 1 + kind, h:h + 1], in1=part,
                        op0=ALU.mult, op1=ALU.add)
                    ins.then_inc(x_added if kind else fox_added, 1)

            def new_xT(cb):
                dve.wait_ge(xt_full, 2 * cb + 2)
                nc.vector.tensor_copy(newT[:, 4 * cb + 2:4 * cb + 4, :],
                                      tokens_of(bank[XT_BANK[cb] + 1][:, :])).then_inc(xt_moved_dve, 1)

            for i in range(SLOTS_OUT):
                if i in (12, 14):
                    new_xT(i // 2 - 6)
                if i < 6:
                    attend(HEAD_GROUPS, i, 0)
                if 2 * i + 4 < 2 * SLOTS_OUT:
                    low(HEAD_GROUPS, 2 * i + 4)
                if i < 6:
                    attend(HEAD_GROUPS, i, 1)
                if 2 * i + 5 < 2 * SLOTS_OUT:
                    low(HEAD_GROUPS, 2 * i + 5)
                if i < 6:
                    attend(HEAD_GROUPS, i, 2)
                if i in (1, 8):
                    dve.wait_ge(sums_full, 1 + i // 8)
                    rsqrt(2 + i // 8, bank[5 if i == 1 else 7][:, 256:258], D // 2)
                    dve.sem_inc(sums_read, 1)
                if i in (2, 4, 6, 8):
                    add_out(0, i // 2 - 1)
                if i == 15:
                    new_xT(2)
                if i in (9, 11, 13, 15):
                    add_out(1, (i - 9) // 2)
            new_xT(3)
            dve.wait_ge(squares, HALF + 8)
            own(nc.vector.tensor_reduce(ssq[:, 10:12], ssq[:, 2:10].rearrange("p (h c) -> p h c", h=HALF),
                                        AX.X, ALU.add))

            def move_parts():
                dve.wait_ge(parts_ready, 1)
                nc.vector.tensor_copy(hid[:, 0:T], bank[4][:, 0:T]).then_inc(parts_moved, 1)

            rsqrt(4, ssq[:, 10:12], D, beside=move_parts)

            TT, TR = nc.vector.tensor_tensor, nc.vector.tensor_reduce
            ALL4 = [P, HALF, NG, EG]

            def by_group(v):
                return v.rearrange("p h (g e) -> p h g e", g=NG)

            def step(*together):
                own(together[-1])

            def per_group(v):
                return v.unsqueeze(3).to_broadcast(ALL4)

            ramp4 = ramp.unsqueeze(1).to_broadcast([P, HALF, NG])
            ramp44 = ramp.unsqueeze(1).unsqueeze(1).to_broadcast(ALL4)
            lg, le = rt[:, :, 0:4], by_group(rt[:, :, 4:20])
            best1, best2, first = rt[:, :, 40:44], rt[:, :, 44:48], rt[:, :, 48:52]
            hit, hot1, hot2, rest = (by_group(rt[:, :, n:n + NE]) for n in (52, 68, 84, 100))
            g_best, g_hit, g_first, g_hot = rt[:, :, 116:117], rt[:, :, 120:124], rt[:, :, 117:118], rt[:, :, 124:128]
            g_sum, e_sum = rt[:, :, 118:119], rt[:, :, 128:132]
            exp_g, exp_e = less[:, :, 0:4], by_group(less[:, :, 4:20])
            wide_mask, weight = by_group(mask[:, :, :]), by_group(comb[:, :, 0:NE])

            def per_half(v, n=NG):
                return v.to_broadcast([P, HALF, n])

            dve.wait_ge(routed_pe, 1)
            for h in range(HALF):
                last = nc.vector.scalar_tensor_tensor(
                    out=rt[:, h, 0:20], in0=bank[5][:, h * QUAD:h * QUAD + NG + NE], scalar=rs[:, 3, h:h + 1],
                    in1=of("rb")[:, h * (NG + NE):(h + 1) * (NG + NE)], op0=ALU.mult, op1=ALU.add)
            own(last)
            step(TR(best1, le, AX.X, ALU.max), TR(g_best, lg, AX.X, ALU.max))
            step(TT(hit, le, per_group(best1), ALU.is_equal), TT(g_hit, lg, per_half(g_best), ALU.is_equal))
            step(TT(hit, hit, ramp44, ALU.mult), TT(g_hit, g_hit, ramp4, ALU.mult))
            step(TR(first, hit, AX.X, ALU.max), TR(g_first, g_hit, AX.X, ALU.max))
            step(TT(hot1, hit, per_group(first), ALU.is_equal), TT(g_hot, g_hit, per_half(g_first), ALU.is_equal))
            for h in range(HALF):
                last = nc.vector.scalar_tensor_tensor(
                    out=rt[:, h, 100:116], in0=rt[:, h, 68:84], scalar=NEG, in1=rt[:, h, 4:20], op0=ALU.mult,
                    op1=ALU.add)
            own(last)
            step(TR(best2, rest, AX.X, ALU.max))
            step(TT(hit, rest, per_group(best2), ALU.is_equal))
            step(TT(hit, hit, ramp44, ALU.mult))
            step(TR(first, hit, AX.X, ALU.max))
            step(TT(hot2, hit, per_group(first), ALU.is_equal))
            step(TT(hot1, hot1, hot2, ALU.add))
            TT(wide_mask, hot1, per_group(g_hot), ALU.mult).then_inc(small_dve, 1)

            TT(exp_e, le, per_group(best1), ALU.subtract)
            TT(exp_g, lg, per_half(g_best), ALU.subtract).then_inc(small_dve, 1)
            dve.wait_ge(small_act, 2)
            step(TR(e_sum, exp_e, AX.X, ALU.add), TR(g_sum, exp_g, AX.X, ALU.add))
            step(nc.vector.reciprocal(e_sum, e_sum), nc.vector.reciprocal(g_sum, g_sum))
            step(TT(exp_e, exp_e, per_group(e_sum), ALU.mult))
            step(TT(exp_e, exp_e, hot1, ALU.mult))

            dve.wait_ge(routed_pe, 2)
            ranks = bank[1][:, 0:HALF * NE].rearrange("p (h e) -> p h e", h=HALF)
            TR(cmax[:, 1:2], bank[1][:, 2 * NE:3 * NE], AX.X, ALU.max)
            own(nc.vector.scalar_tensor_tensor(out=pos[:, :, 0:NE], in0=ranks, scalar=1.0, in1=mask[:, :, :],
                                               op0=ALU.add, op1=ALU.mult))
            own(nc.vector.tensor_scalar(pos[:, :, 0:NE], pos[:, :, 0:NE], -1.0, None, ALU.add))

            def pick(dst, pair, ready):
                for half in range(HALF):
                    for e in range(2):
                        n = 2 * pair + e
                        n = slice(n, n + 1) if isinstance(n, int) else bass.ds(n, 1)
                        weight = rs[:, 3, half:half + 1] if dst is pickD else comb[:, half, n]
                        last = nc.vector.tensor_scalar(dst[:, half, e * CAP:(e + 1) * CAP], window, pos[:, half, n],
                                                       weight, ALU.is_equal, ALU.mult)
                last.then_inc(ready, 1)

            pick(pickD, 0, pickD_ready)
            own(nc.vector.tensor_scalar(cmax[:, 2:5], of("steps")[:, 0:3], cmax[:, 1:2], None, ALU.is_lt))
            own(TR(cmax[:, 5:6], cmax[:, 2:5], AX.X, ALU.add))
            nc.vector.tensor_scalar(n_pass[:, :], cmax[0:1, 5:6], 1.0, None, ALU.add).then_inc(pass_ready, 1)
            step(TR(e_sum, exp_e, AX.X, ALU.add))
            step(nc.vector.reciprocal(e_sum, e_sum))
            step(TT(e_sum, e_sum, g_hot, ALU.mult))
            step(TT(e_sum, e_sum, per_half(g_sum), ALU.mult))
            step(TT(weight, exp_e, per_group(e_sum), ALU.mult),
                 nc.vector.tensor_scalar(pos[:, :, NE:], pos[:, :, 0:2], -float(CAP), None, ALU.add))
            step(nc.vector.tensor_copy(comb[:, :, NE:], comb[:, :, 0:2]))

            def pair(q, i, first=False):
                base = q * SLOTS_PAIR
                for c in range(4):
                    dve.wait_ge(g_full, 4 * q + c + 1)
                    nc.vector.tensor_tensor(
                        xeT[:, 4 * c:4 * c + 4, :],
                        bank[GATHER_BANKS[c]][:, :].rearrange("p (k s) -> p k s", k=4),
                        gT[:, 2 * KD + 4 * c:2 * KD + 4 * c + 4].unsqueeze(2).to_broadcast([P, 4, P]),
                        ALU.mult).then_inc(g_moved, 1)
                dve.wait_ge(wt_full, FREE + q)
                pick(pickW, i, pickW_ready)
                if not first:
                    dve.wait_ge(y_begun, HALF)
                    for n in range(8):
                        cb, h = divmod(n, HALF)
                        dve.wait_ge(scat_full, SCATTERS * q + n + 1)
                        part = y_sum[:, h, cb * 512:(cb + 1) * 512]
                        nc.vector.tensor_tensor(part, part, bank[7 - n % 2][:, :], ALU.add).then_inc(scat_moved, 1)
                dve.wait_ge(wt_full, FREE + q + 1)
                nc.vector.tensor_copy(pickWT[:, :], bank[2][:, 0:T]).then_inc(wt_moved, 1)
                dve.wait_ge(gate_read, FREE + q + 1)
                dve.wait_ge(moe_used, base + 16)
                nc.vector.tensor_tensor(hid[:, :], sg[:, :], bank[1][:, :], ALU.mult).then_inc(hid_ready, 1)
                pick(pickD, i + 1, pickD_ready)
                for cb in range(2, 4):
                    if cb == 2:
                        dve.wait_ge(down_full, 3 * q + cb + 1)
                    else:
                        dve.wait_ge(moe_used, base + SLOTS_PAIR)
                    nc.vector.tensor_copy(y_slots[:, cb * 512:(cb + 1) * 512],
                                          bank[2 + cb][:, :]).then_inc(y_moved_dve, 1)

            def next_window(p):
                nc.vector.tensor_scalar(window, window, float(CAP), None, ALU.add).then_inc(window_ready, 1)
                dve.wait_ge(window_ready, p + 1)

            pair(0, 0, True)
            with dve.Fori(1, PAIRS) as i:
                pair(i, i)
            next_window(0)
            dve.wait_ge(pass_ready, 1)
            passes = dve.value_load(n_pass[0:1, 0:1], min_val=1, max_val=T // CAP)
            with dve.If(passes > 1):
                with dve.Fori(1, passes) as p:
                    with dve.Fori(0, PAIRS) as i:
                        pair(p * PAIRS + i, i)
                    next_window(p)

            def add_last(n):
                h, cb = n // 4, n % 4
                dve.wait_ge(scat_full, passes * (SCATTERS * PAIRS) + n + 1)
                part = y_sum[:, h, cb * 512:(cb + 1) * 512]
                nc.vector.tensor_tensor(part, part, bank[LAST_BANKS[n % 4]][:, :], ALU.add).then_inc(scat_moved, 1)

            def total(h):
                dve.wait_ge(squares, HALF + 8 + 4 * (h + 1))
                own(nc.vector.tensor_reduce(ssq[:, 20 + h:21 + h], ssq[:, 12 + 4 * h:16 + 4 * h], AX.X, ALU.add))

            def finish(h, part):
                cols = slice(part * (D // 2), (part + 1) * (D // 2))
                nc.vector.scalar_tensor_tensor(out=x[:, h, cols], in0=y_sum[:, h, cols], scalar=rs[:, 4, h:h + 1],
                                               in1=gfin[:, cols], op0=ALU.mult, op1=ALU.mult).then_inc(out_ready, 1)

            for n in range(6):
                add_last(n)
            total(0)
            rsqrt(5, ssq[:, 20:21], D, row=4, cols=slice(0, 1), beside=lambda: add_last(6))
            add_last(7)
            dve.wait_ge(gfin_loaded, 16)
            finish(0, 0)
            total(1)
            rsqrt(6, ssq[:, 21:22], D, row=4, cols=slice(1, 2), beside=lambda: finish(0, 1))
            finish(1, 0)
            finish(1, 1)

        @block.tensor
        def _(pe):
            for s in (pv_full, wt_full, t_full):
                pe.sem_inc(s, FREE)
            pe.sem_inc(scat_full, SCATTERS)

            def split_product(dst, lhs, rhs, k, cols, rhs_of, first, last):
                hi, lo = lhs[0][:, k, cols], lhs[1][:, k, cols]
                nc.tensor.matmul(dst, hi, rhs_of(rhs[0]), start=first, stop=False)
                nc.tensor.matmul(dst, hi, rhs_of(rhs[1]), start=False, stop=False)
                return nc.tensor.matmul(dst, lo, rhs_of(rhs[0]), start=False, stop=last)

            def half_product(h, n, lhs, dst, k0, k_first, k_last):
                pe.wait_ge(halves_split, 2 * SLOTS_QKV * h + n + 1)
                for half in range(HALF):
                    for kk in range(2):
                        last = split_product(bank[dst + half][:, :], lhs, (w_hi, w_lo), k0 + kk,
                                             slice(half * P, (half + 1) * P),
                                             lambda w, kk=kk: w[:, n % SPLITS, kk * 512:(kk + 1) * 512],
                                             k0 + kk == k_first, k0 + kk == k_last)
                last.then_inc(halves_used, 1)

            def narrow_product(dst, tokens, w, n, ks, first, last):
                for k in ks:
                    quad = slice(k % 4 * QUAD, (k % 4 + 1) * QUAD)
                    ins = nc.tensor.matmul(dst[quad, 0:T], w[:, k * n:k * n + QUAD], tokens[:, k, :],
                                           start=k < first + 4, stop=k > last - 4)
                return ins

            def add_quarters(dst, parts, n):
                for half in range(HALF):
                    ins = nc.tensor.matmul(dst[:, half * QUAD:half * QUAD + n], parts[:, half * P:(half + 1) * P],
                                           of("add4")[:, 0:n], start=True, stop=True)
                return ins

            pe.wait_ge(first_loaded, 16)
            nc.tensor.matmul(bank[7][0:HEADS, 0:384], of("relT", BUCKETS + 1), of("onehot", BUCKETS + 1), start=True,
                             stop=True).then_inc(small_pe, 1)

            def attend(h, s):
                g = h - 1

                def scores(a):
                    if a == 0:
                        pe.wait_ge(q_moved, 2 * h)
                        pe.wait_ge(k_moved, 2 * h)
                    pe.wait_ge(s_moved, FREE + 4 * g + a)
                    for qt in range(HALF):
                        dst = bank[6][:, 0:P] if qt == 0 else bank[6][:, P:3 * P]
                        n = (qt + 1) * P
                        last = nc.tensor.matmul(dst, qT[:, a, qt * P:n], kT[:, a, 0:n], start=True, stop=True)
                    last.then_inc(s_full, 1)

                def values(a):
                    pe.wait_ge(t_moved, FREE + 4 * g + a + 1)
                    pe.wait_ge(v_moved, 2 * h)
                    if a >= 2:
                        pe.wait_ge(o_moved, FREE + 4 * g + a - 1)
                    dst, v = bank[4 + a % 2], v_tok[:, :, a * HD:(a + 1) * HD]
                    nc.tensor.matmul(dst[:, 0:T], v[:, 0], prT[:, 0:T], start=True, stop=False)
                    nc.tensor.matmul(dst[:, P:T], v[:, 1], prT[:, T:T + P], start=False,
                                     stop=True).then_inc(pv_full, 1)

                def turn(a):
                    pe.wait_ge(pr_ready, FREE + 2 * (4 * g + a) + 2)
                    pe.wait_ge(t_moved, FREE + 4 * g + a)
                    for n in range(3):
                        last = nc.tensor.transpose(bank[7][:, n * P:(n + 1) * P], pr[:, n * P:(n + 1) * P], ident)
                    last.then_inc(t_full, 1)

                if s < 4:
                    scores(s)
                if 2 <= s < 6:
                    values(s - 2)
                if 1 <= s < 5:
                    turn(s - 1)

            def turned_product(h, n, dst, k0):
                pe.wait_ge(halves_split, 2 * SLOTS_QKV * h + n + 1)
                for kk in range(2):
                    k = k0 + kk
                    for a in range(GROUP_H):
                        to = bank[dst + a // 2][:, a % 2 * T:(a % 2 + 1) * T]
                        hi, lo = (w[:, n % SPLITS, kk * 512 + a * HD:kk * 512 + (a + 1) * HD] for w in (w_hi, w_lo))
                        nc.tensor.matmul(to, hi, hT_hi[:, k, :], start=k == 0 and a % 2 == 0, stop=False,
                                         skip_group_check=True)
                        nc.tensor.matmul(to, hi, hT_lo[:, k, :], start=False, stop=False, skip_group_check=True)
                        last = nc.tensor.matmul(to, lo, hT_hi[:, k, :], start=False, stop=k == KD - 1,
                                                skip_group_check=True)
                last.then_inc(halves_used, 1)

            def period(h, s, attending):
                b, j = divmod(s, KD // KPS)
                if attending and j == 0:
                    pe.wait_ge((q_moved, k_moved, v_moved)[b], 2 * h)
                    if b == 2:
                        pe.wait_ge(o_moved, FREE + 4 * h)
                for part in range(2):
                    if not attending and b == 0:
                        pe.wait_ge(hT_ready, KPS * j + 2 * part + 2)
                    if b < 2:
                        turned_product(h, 2 * s + part, 2 * b, KPS * j + 2 * part)
                    else:
                        half_product(h, 2 * s + part, (hT_hi, hT_lo), 4, KPS * j + 2 * part, 0, KD - 1)
                if attending:
                    attend(h, s)

            for s in range(SLOTS_QKV):
                if s == 0:
                    pe.wait_ge(small_dve, 1)
                period(0, s, False)
                if s == 3:
                    pe.wait_ge(small_loaded, 16)
                    pe.wait_ge(wsmall_ready, 1)
                    narrow_product(bank[6], xT, wf, FOX, range(KD), 0, KD - 1).then_inc(small_pe, 1)
                if s == 4:
                    pe.wait_ge(small_dve, 2)
                    add_quarters(bank[6][:, T:], sc, FOX).then_inc(small_pe, 1)
                if s == 5:
                    pe.wait_ge(small_dve, 3)
                    nc.tensor.matmul(bank[7][:, 0:T], ones, pr[:, 0:T], start=True, stop=True).then_inc(small_pe, 1)
                if s == 8:
                    pe.wait_ge(small_dve, 5)
                    nc.tensor.matmul(bank[6][0:HEADS, 0:T], lf[:, 0, :], tri_ones, start=True, stop=False)
                    nc.tensor.matmul(bank[6][0:HEADS, P:T], lf[:, 1, :], tri, start=False, stop=True)
                    nc.tensor.matmul(bank[6][:, T:T + HEADS], tri, lf[:, 0, :], start=True, stop=True)
                    nc.tensor.matmul(bank[6][:, T + HEADS:T + 2 * HEADS], ones, lf[:, 0, :], start=True, stop=False)
                    nc.tensor.matmul(bank[6][:, T + HEADS:T + 2 * HEADS], tri, lf[:, 1, :], start=False,
                                     stop=True).then_inc(small_pe, 1)
            pe.wait_ge(small_dve, 6)
            with pe.Fori(1, HEAD_GROUPS) as h:
                for s in range(SLOTS_QKV):
                    period(h, s, True)

            def sums(kind, dst):
                pe.wait_ge(sq_added, 1 + FOX * (kind + 1))
                for half in range(HALF):
                    last = nc.tensor.matmul(dst[:, T + half:T + half + 1], sqs[:, kind, half * P:(half + 1) * P],
                                            ones[:, 0:1], start=True, stop=True)
                last.then_inc(sums_full, 1)

            def new_xT(cb):
                for half in range(HALF):
                    pe.wait_ge(x_added, 2 * cb + (half + 1 if cb else 2))
                    for k in range(4 * cb, 4 * cb + 4):
                        at = k % 2 * T + half * P
                        last = nc.tensor.transpose(bank[XT_BANK[cb] + k % 4 // 2][:, at:at + P],
                                                   x[:, half, k * P:(k + 1) * P], ident)
                        if half and k % 2:
                            last.then_inc(xt_full, 1)

            def route(cb):
                pe.wait_ge(xt_moved_act, cb + 1)
                pe.wait_ge(xt_moved_dve, cb + 1)
                pe.wait_ge(wsmall_ready, 2)
                return narrow_product(bank[4], newT, wr, NG + NE, range(4 * cb, 4 * cb + 4), 0, KD - 1)

            for i, (kind, cb, j) in enumerate(OUT_ORDER):
                dst = OUT_BANKS[kind, cb]
                if j == 2 * kind:
                    if i == 0:
                        pe.wait_ge(q_moved, 2 * HEAD_GROUPS)
                        pe.wait_ge(k_moved, 2 * HEAD_GROUPS)
                    elif (kind, cb) in ((0, 2), (0, 3)):
                        pe.wait_ge(fox_added, 2 * cb - 2)
                    elif (kind, cb) in ((1, 2), (1, 3)):
                        pe.wait_ge(fox_added, 2 * cb + 2)
                    if (kind, cb) == (1, 0):
                        pe.wait_ge(o_moved, FREE + HEADS)
                    if (kind, cb) == (1, 1):
                        pe.wait_ge(sums_read, 2)
                for part in range(2):
                    half_product(HEAD_GROUPS, 2 * i + part, (oT_hi, oT_lo), dst, KPS * j + 2 * part, 8 * kind,
                                 8 * kind + 7)
                if i == 0:
                    pe.wait_ge(v_moved, 2 * HEAD_GROUPS)
                    sums(0, bank[5])
                if i == 7:
                    sums(1, bank[7])
                if i == 3:
                    pe.wait_ge(sums_read, 1)
                if i < 6:
                    attend(HEAD_GROUPS, i)
                if i in (11, 13):
                    new_xT((i - 11) // 2)
                if i in (12, 14):
                    route((i - 12) // 2)
                if i == 14:
                    new_xT(2)
            route(2)
            new_xT(3)
            route(3).then_inc(parts_ready, 1)
            pe.wait_ge(parts_moved, 1)
            add_quarters(bank[5], hid, NG + NE).then_inc(routed_pe, 1)

            pe.wait_ge(small_dve, 7)
            masks = mask[:, :, :].rearrange("p h e -> p (h e)")
            nc.tensor.matmul(bank[1][:, 0:2 * NE], strict, masks, start=True, stop=False, skip_group_check=True)
            nc.tensor.matmul(bank[1][:, NE:3 * NE], ones, masks, start=False, stop=False, skip_group_check=True)
            nc.tensor.matmul(bank[1][:, 2 * NE:3 * NE], ones, mask[:, 0, :], start=False, stop=True,
                             skip_group_check=True).then_inc(routed_pe, 1)

            def pair(body, u, first=False):
                q = body * 2 + u
                at_once = first and u == 0

                def landed(j):
                    to, loaded, turn = moe_slot(u * SLOTS_PAIR + j, first)
                    pe.wait_ge(loaded, 16 * (turn + 1) + body * (16 * 2 * SLOTS_PAIR // MOE_RING))
                    return to

                def gather(c):
                    if c == 0:
                        pe.wait_ge(pickD_ready, q + 1)
                    if c == 2:
                        pe.wait_ge(y_moved_dve, FREE + 2 * q)
                    for k in range(4):
                        for half in range(HALF):
                            kd = 4 * c + k
                            last = nc.tensor.matmul(bank[GATHER_BANKS[c]][:, k * P:(k + 1) * P],
                                                    x[:, half, kd * P:(kd + 1) * P], pickD[:, half, :],
                                                    start=(half == 0), stop=(half == HALF - 1))
                    last.then_inc(g_full, 1)

                gather(0)
                for m in range(2):
                    for j in range(KD // KPS):
                        if m == 0:
                            for c in (((), (1, 2), (3,), ()) if at_once else ((1,), (2,), (3,), ()))[j]:
                                gather(c)
                        if m == 0:
                            pe.wait_ge(g_moved, 4 * q + j + 1)
                        if j == 0:
                            pe.wait_ge((gate_read, hid_ready)[m], FREE + q)
                        at = 2 * (m * (KD // KPS) + j)
                        s = [landed(at + e) for e in range(2)]
                        for k in range(KPS):
                            kd = KPS * j + k
                            for e in range(2):
                                last = nc.tensor.matmul(bank[m][e * CAP:(e + 1) * CAP, :],
                                                        xeT[:, kd, e * CAP:(e + 1) * CAP],
                                                        s[e][:, k * 512:(k + 1) * 512],
                                                        start=(kd == 0), stop=(kd == KD - 1))
                                if k == KPS - 1:
                                    last.then_inc(moe_used, 1)
                    if m == 0 and not at_once:
                        pe.wait_ge(y_moved_act, FREE + 2 * q)
                        for n in range(8):
                            cb, half = divmod(n, HALF)
                            if n >= 2:
                                pe.wait_ge(scat_moved, SCATTERS * q + n - 1)
                            nc.tensor.matmul(bank[7 - n % 2][:, :], pickWT[:, half * P:(half + 1) * P],
                                             y_slots[:, cb * 512:(cb + 1) * 512], start=True,
                                             stop=True).then_inc(scat_full, 1)
                    if m == 0:
                        pe.wait_ge(pickW_ready, q + 1)
                        for half in range(HALF):
                            last = nc.tensor.transpose(bank[2][:, half * P:(half + 1) * P], pickW[:, half, :], ident)
                        last.then_inc(wt_full, 1)

                pe.wait_ge(hid_ready, FREE + q + 1)
                for k in range(KF):
                    last = nc.tensor.transpose(bank[6][:, k * P:(k + 1) * P], hid[:, k * P:(k + 1) * P], ident)
                last.then_inc(hidT_full, 1)
                pe.wait_ge(hidT_moved, q + 1)
                pe.wait_ge(wt_moved, q + 1)
                for k in range(KF):
                    s = [landed(2 * (2 * KD // KPS + k) + e) for e in range(2)]
                    for cb in range(4):
                        for e in range(2):
                            if k == KF - 1 and cb == 2:
                                pe.wait_ge(late_in[e], 16 * (q + 1))
                            last = nc.tensor.matmul(bank[2 + cb][e * CAP:(e + 1) * CAP, :],
                                                    hidT[:, k, e * CAP:(e + 1) * CAP],
                                                    s[e][:, cb * 512:(cb + 1) * 512],
                                                    start=(k == 0), stop=(k == KF - 1))
                            if cb == 3:
                                last.then_inc(moe_used, 1)
                        if k == KF - 1 and cb < 3:
                            last.then_inc(down_full, 1)

            for u in range(2):
                pair(0, u, True)
            pe.wait_ge(pass_ready, 1)
            passes = pe.value_load(n_pass[0:1, 0:1], min_val=1, max_val=T // CAP)
            with pe.Fori(1, passes * (PAIRS // 2)) as body:
                for u in range(2):
                    pair(body, u)

            pairs = passes * PAIRS
            for n in range(8):
                half, cb = n // 4, n % 4
                if n < 4:
                    pe.wait_ge((y_moved_act, y_moved_dve)[cb // 2], FREE + 2 * pairs - 1 + cb % 2)
                else:
                    pe.wait_ge(scat_moved, SCATTERS * pairs + n - 3)
                nc.tensor.matmul(bank[LAST_BANKS[n % 4]][:, :], pickWT[:, half * P:(half + 1) * P],
                                 y_slots[:, cb * 512:(cb + 1) * 512], start=True, stop=True).then_inc(scat_full, 1)


def kernel(**inputs):
    import concourse.bacc as bacc
    from concourse.bass_utils import run_bass_kernel_spmd

    nc = bacc.Bacc("TRN2", target_bir_lowering=False, num_devices=1)
    i = {n: np.asarray(a) for n, a in inputs.items()}
    arrays = {
        "x": i["x"],
        "xT": i["x"][0].T.reshape(KD, P, T).transpose(1, 0, 2),
        "small": small_table(i),
        "w_in": i["w_in"], "w_out": i["w_out"], "w_gate": i["w_gate"], "w_up": i["w_up"], "w_down": i["w_down"],
        "g_final": i["final_norm_g"],
    }
    arrays = {f"in_{n}": np.ascontiguousarray(a) for n, a in arrays.items()}
    args = [nc.dram_tensor(n, a.shape, mybir.dt.from_np(a.dtype), kind="ExternalInput").ap()
            for n, a in arrays.items()]
    args.append(nc.dram_tensor("out", i["x"].shape, F32, kind="ExternalOutput").ap())
    layer(nc, *args)
    r = run_bass_kernel_spmd(nc, [arrays], core_ids=[0])
    return r.results[0]["out"]
```
